# Optimizing a Trainium2 kernel written in Bass

```python
import jax, jax.numpy as jnp
from jax import lax
import numpy as np

D_MODEL = 1024
BATCH = 1
SEQ = 512
DEPTH = 1
DEC_BATCH = 8
DEC_SEQ = 4
PAST_LEN = 2048
PAGE_SIZE = 128

HEAD_DIM = 64
NSA_HEADS = 8
NSA_KV_HEADS = 2
NSA_REP = NSA_HEADS // NSA_KV_HEADS
CMP_STRIDE = 16
CMP_BLOCK = 2 * CMP_STRIDE
CMP_HIDDEN = 2 * HEAD_DIM
SEL_BLOCK = 64
SEL_TOPN = 16
NSA_WINDOW = 512
NSA_QBLOCK = 64
DIL_HEADS = 4
DIL_CONFIGS = ((128, 1), (512, 4), (2048, 16))
N_DIL = 3
DIL_QBLOCK = 128
ROPE_THETA = 500000.0
ROPE_DIM = HEAD_DIM // 4
N_GROUPS = 4
EXPERTS_PER_GROUP = 8
N_EXPERTS = N_GROUPS * EXPERTS_PER_GROUP
EXPERT_TOPK = 2
EXPERT_FF = 256
MOE_BLOCK = 128
RMS_EPS = 1e-6

NSA_Q_DIM = NSA_HEADS * HEAD_DIM
NSA_KV_DIM = NSA_KV_HEADS * HEAD_DIM
DIL_DIM = DIL_HEADS * HEAD_DIM
SPLIT_POINTS = (NSA_Q_DIM,
                NSA_Q_DIM + 6 * NSA_KV_DIM,
                NSA_Q_DIM + 6 * NSA_KV_DIM + 3 * NSA_HEADS,
                NSA_Q_DIM + 6 * NSA_KV_DIM + 3 * NSA_HEADS + 3 * N_DIL * DIL_DIM)
IN_DIM = SPLIT_POINTS[3] + 2 * D_MODEL

kernel_name = 'nsa_dilated_hier_moe_decode_step'

def rms_norm(x, g):
    xf = x.astype(jnp.float32)
    inv = lax.rsqrt(jnp.mean(xf * xf, axis=-1, keepdims=True) + RMS_EPS)
    return (xf * inv * g.astype(jnp.float32)).astype(x.dtype)

def rope_partial(x, pos):
    half = ROPE_DIM // 2
    inv_freq = 1.0 / (ROPE_THETA ** (jnp.arange(half, dtype=jnp.float32) * (2.0 / ROPE_DIM)))
    ang = pos.astype(jnp.float32)[:, None] * inv_freq[None, :]
    cos = jnp.cos(ang)[:, None, :]
    sin = jnp.sin(ang)[:, None, :]
    xf = x.astype(jnp.float32)
    x1 = xf[..., :half]
    x2 = xf[..., half:ROPE_DIM]
    out = jnp.concatenate([x1 * cos - x2 * sin, x2 * cos + x1 * sin, xf[..., ROPE_DIM:]], axis=-1)
    return out.astype(x.dtype)

def masked_softmax(s, mask):
    s = jnp.where(mask, s.astype(jnp.float32), -jnp.inf)
    m = jnp.max(s, axis=-1, keepdims=True)
    m = jnp.where(jnp.isfinite(m), m, 0.0)
    e = jnp.exp(s - m)
    den = jnp.sum(e, axis=-1, keepdims=True)
    p = e / jnp.where(den > 0, den, 1.0)
    lse = (m + jnp.log(den))[..., 0]
    return p, lse

def compress_kv(k, pe, w1, w2):
    b, t, g, d = k.shape
    n_chunk = t // CMP_STRIDE
    kc = k[:, :n_chunk * CMP_STRIDE].reshape(b, n_chunk, CMP_STRIDE, g, d)
    blocks = jnp.concatenate([kc[:, :-1], kc[:, 1:]], axis=2) + pe[None, None, :, None, :]
    flat = blocks.transpose(0, 1, 3, 2, 4).reshape(b, n_chunk - 1, g, CMP_BLOCK * d)
    return jax.nn.gelu(flat @ w1) @ w2

def selection_blocks(k, n_sel):
    b, t, g, d = k.shape
    k = jnp.pad(k, ((0, 0), (0, n_sel * SEL_BLOCK - t), (0, 0), (0, 0)))
    return k.reshape(b, n_sel, SEL_BLOCK, g, d).transpose(0, 3, 1, 2, 4)

def cover_matrix(n_cmp, n_sel):
    start = jnp.arange(n_cmp) * CMP_STRIDE
    j0 = jnp.arange(n_sel) * SEL_BLOCK
    hit = (start[:, None] < j0[None, :] + SEL_BLOCK) & (start[:, None] + CMP_BLOCK > j0[None, :])
    return hit.astype(jnp.float32)

def nsa_context(k_cmp_raw, v_cmp_raw, k_sel, v_sel, cmp_w):
    pe_k, w1_k, w2_k, pe_v, w1_v, w2_v = cmp_w
    k_cmp = compress_kv(k_cmp_raw, pe_k, w1_k, w2_k)
    v_cmp = compress_kv(v_cmp_raw, pe_v, w1_v, w2_v)
    n_cmp = k_cmp.shape[1]
    cmp_end = jnp.arange(n_cmp) * CMP_STRIDE + (CMP_BLOCK - 1)
    t = k_sel.shape[1]
    n_sel = max(-(-t // SEL_BLOCK), SEL_TOPN)
    ks_blk = selection_blocks(k_sel, n_sel)
    vs_blk = selection_blocks(v_sel, n_sel)
    return k_cmp, v_cmp, cmp_end, ks_blk, vs_blk, cover_matrix(n_cmp, n_sel)

def nsa_attend(q_rot, q_raw, q_pos, k_cmp, v_cmp, cmp_end, ks_blk, vs_blk, cover, k_win, v_win, win_pos, gate):
    b, tq, h, d = q_rot.shape
    scale = d ** -0.5
    qr = q_rot.reshape(b, tq, NSA_KV_HEADS, NSA_REP, d)
    qc = q_raw.reshape(b, tq, NSA_KV_HEADS, NSA_REP, d)
    s = jnp.einsum('bqgrd,bcgd->bgrqc', qc, k_cmp) * scale
    p_cmp, _ = masked_softmax(s, cmp_end[None, :] <= q_pos[:, None])
    o_cmp = jnp.einsum('bgrqc,bcgd->bqgrd', p_cmp.astype(v_cmp.dtype), v_cmp)
    imp = jnp.einsum('bgrqc,cn->bgqn', p_cmp, cover)
    n_sel = cover.shape[1]
    blk = jnp.arange(n_sel)[None, :]
    cur = (q_pos // SEL_BLOCK)[:, None]
    eligible = blk <= cur
    forced = (blk == 0) | (blk == cur) | (blk == cur - 1)
    score = jnp.where(eligible, jnp.where(forced, jnp.inf, imp), -jnp.inf)
    top_val, top_idx = lax.top_k(score, SEL_TOPN)
    bi = jnp.arange(b)[:, None, None, None]
    gi = jnp.arange(NSA_KV_HEADS)[None, :, None, None]
    ks = ks_blk[bi, gi, top_idx]
    vs = vs_blk[bi, gi, top_idx]
    key_pos = top_idx[..., None] * SEL_BLOCK + jnp.arange(SEL_BLOCK)
    sel_mask = (top_val > -jnp.inf)[..., None] & (key_pos <= q_pos[None, None, :, None, None])
    s = jnp.einsum('bqgrd,bgqnkd->bgrqnk', qr, ks) * scale
    s = s.reshape(b, NSA_KV_HEADS, NSA_REP, tq, SEL_TOPN * SEL_BLOCK)
    p_sel, _ = masked_softmax(s, sel_mask.reshape(b, NSA_KV_HEADS, 1, tq, SEL_TOPN * SEL_BLOCK))
    o_sel = jnp.einsum('bgrqk,bgqkd->bqgrd', p_sel.astype(vs.dtype),
                       vs.reshape(b, NSA_KV_HEADS, tq, SEL_TOPN * SEL_BLOCK, d))
    s = jnp.einsum('bqgrd,bkgd->bgrqk', qr, k_win) * scale
    dist = q_pos[:, None] - win_pos[None, :]
    p_win, _ = masked_softmax(s, (win_pos[None, :] >= 0) & (dist >= 0) & (dist < NSA_WINDOW))
    o_win = jnp.einsum('bgrqk,bkgd->bqgrd', p_win.astype(v_win.dtype), v_win)
    gt = gate.reshape(b, tq, NSA_KV_HEADS, NSA_REP, 3)
    o = gt[..., 0:1] * o_cmp + gt[..., 1:2] * o_sel + gt[..., 2:3] * o_win
    return o.reshape(b, tq, h * d)

def nsa_prompt(q_rot, q_raw, ctx, k_win, v_win, gate):
    b, t, h, d = q_rot.shape
    nb = t // NSA_QBLOCK
    pad = ((0, 0), (NSA_WINDOW, 0), (0, 0), (0, 0))
    kw = jnp.pad(k_win, pad)
    vw = jnp.pad(v_win, pad)
    span = NSA_QBLOCK + NSA_WINDOW

    def to_blocks(a):
        return a.reshape(b, nb, NSA_QBLOCK, *a.shape[2:]).swapaxes(0, 1)

    def body(args):
        qr, qc, gt, start = args
        q_pos = start + jnp.arange(NSA_QBLOCK)
        kwb = lax.dynamic_slice_in_dim(kw, start, span, axis=1)
        vwb = lax.dynamic_slice_in_dim(vw, start, span, axis=1)
        win_pos = start - NSA_WINDOW + jnp.arange(span)
        return nsa_attend(qr, qc, q_pos, *ctx, kwb, vwb, win_pos, gt)

    out = lax.map(body, (to_blocks(q_rot), to_blocks(q_raw), to_blocks(gate),
                         jnp.arange(nb, dtype=jnp.int32) * NSA_QBLOCK))
    return out.swapaxes(0, 1).reshape(b, t, h * d)

def dilated_prompt(q, k, v, window, dil):
    b, t, h, d = q.shape
    span = window // dil
    n_res = t // dil
    nb = -(-n_res // DIL_QBLOCK)
    lp = nb * DIL_QBLOCK

    def residues(a):
        return a.reshape(b, n_res, dil, h, d).transpose(0, 2, 1, 3, 4)

    qr = jnp.pad(residues(q), ((0, 0), (0, 0), (0, lp - n_res), (0, 0), (0, 0)))
    kr = jnp.pad(residues(k), ((0, 0), (0, 0), (span, lp - n_res), (0, 0), (0, 0)))
    vr = jnp.pad(residues(v), ((0, 0), (0, 0), (span, lp - n_res), (0, 0), (0, 0)))
    idx = jnp.arange(nb)[:, None] * DIL_QBLOCK + jnp.arange(DIL_QBLOCK + span)[None, :]
    kw = kr[:, :, idx]
    vw = vr[:, :, idx]
    qb = qr.reshape(b, dil, nb, DIL_QBLOCK, h, d)
    s = jnp.einsum('brnqhe,brnkhe->brnhqk', qb, kw) * (d ** -0.5)
    m_q = jnp.arange(nb)[:, None] * DIL_QBLOCK + jnp.arange(DIL_QBLOCK)[None, :]
    m_k = idx - span
    diff = m_q[:, :, None] - m_k[:, None, :]
    mask = (m_k[:, None, :] >= 0) & (diff >= 0) & (diff <= span)
    p, lse = masked_softmax(s, mask[None, None, :, None])
    o = jnp.einsum('brnhqk,brnkhe->brnqhe', p.astype(v.dtype), vw)
    o = o.reshape(b, dil, lp, h, d)[:, :, :n_res].transpose(0, 2, 1, 3, 4).reshape(b, t, h, d)
    lse = lse.transpose(0, 1, 2, 4, 3).reshape(b, dil, lp, h)[:, :, :n_res]
    lse = lse.transpose(0, 2, 1, 3).reshape(b, t, h)
    return o, lse

def dilated_sample(q, k_all, v_all, n_buf, window, dil):
    s_len = q.shape[1]
    span = window // dil
    idx = n_buf + jnp.arange(s_len)[:, None] - dil * jnp.arange(span + 1)[None, :]
    valid = idx >= 0
    idx = jnp.maximum(idx, 0)
    kg = k_all[:, idx]
    vg = v_all[:, idx]
    s = jnp.einsum('bqhe,bqkhe->bhqk', q, kg) * (q.shape[-1] ** -0.5)
    p, lse = masked_softmax(s, valid[None, None])
    o = jnp.einsum('bhqk,bqkhe->bqhe', p.astype(vg.dtype), vg)
    return o, lse.transpose(0, 2, 1)

def combine_dilations(outs, lses):
    w = jax.nn.softmax(jnp.stack(lses, axis=-1), axis=-1)
    o = jnp.einsum('bthn,bthnd->bthd', w.astype(outs[0].dtype), jnp.stack(outs, axis=-2))
    return o.reshape(o.shape[0], o.shape[1], -1)

def project_mixer_inputs(h, pos, w_in):
    b, t, _ = h.shape
    q_nsa, kv_nsa, g_nsa, qkv_dil, g_mrg = jnp.split(h @ w_in, SPLIT_POINTS, axis=-1)
    q_raw = q_nsa.reshape(b, t, NSA_HEADS, HEAD_DIM)
    kv = kv_nsa.reshape(b, t, 6, NSA_KV_HEADS, HEAD_DIM)
    nsa = (rope_partial(q_raw, pos), q_raw, kv[:, :, 0], kv[:, :, 1], rope_partial(kv[:, :, 2], pos),
           kv[:, :, 3], rope_partial(kv[:, :, 4], pos), kv[:, :, 5],
           jax.nn.sigmoid(g_nsa).reshape(b, t, NSA_HEADS, 3))
    qkv = qkv_dil.reshape(b, t, N_DIL, 3, DIL_HEADS, HEAD_DIM)
    dil = [(rope_partial(qkv[:, :, g, 0], pos), rope_partial(qkv[:, :, g, 1], pos), qkv[:, :, g, 2])
           for g in range(N_DIL)]
    merge = jax.nn.sigmoid(g_mrg).reshape(b, t, 2, D_MODEL)
    return nsa, dil, merge

def hier_moe(h, wg, bg, we, be, w_up, w_down):
    n, d = h.shape
    g_logits = (h @ wg).astype(jnp.float32) + bg.astype(jnp.float32)
    g_prob = jax.nn.softmax(g_logits, axis=-1)
    grp = jnp.argmax(g_logits, axis=-1)
    p_grp = jnp.take_along_axis(g_prob, grp[:, None], axis=-1)
    e_logits = ((h @ we).astype(jnp.float32) + be.astype(jnp.float32)).reshape(n, N_GROUPS, EXPERTS_PER_GROUP)
    e_logits = jnp.take_along_axis(e_logits, grp[:, None, None], axis=1)[:, 0]
    top_p, top_i = lax.top_k(jax.nn.softmax(e_logits, axis=-1), EXPERT_TOPK)
    top_p = top_p / jnp.sum(top_p, axis=-1, keepdims=True)
    expert = grp[:, None] * EXPERTS_PER_GROUP + top_i
    weight = p_grp * top_p
    m = n * EXPERT_TOPK
    e_flat = expert.reshape(m)
    order = jnp.argsort(e_flat)
    e_sorted = e_flat[order]
    tok_sorted = (order // EXPERT_TOPK).astype(jnp.int32)
    w_sorted = weight.reshape(m)[order]
    counts = jnp.zeros((N_EXPERTS,), jnp.int32).at[e_flat].add(1)
    starts = jnp.cumsum(counts) - counts
    pcounts = (counts + MOE_BLOCK - 1) // MOE_BLOCK * MOE_BLOCK
    pends = jnp.cumsum(pcounts)
    pstarts = pends - pcounts
    dest = pstarts[e_sorted] + (jnp.arange(m) - starts[e_sorted])
    n_blocks = -(-m // MOE_BLOCK) + N_EXPERTS
    tok_buf = jnp.zeros((n_blocks * MOE_BLOCK,), jnp.int32).at[dest].set(tok_sorted)
    w_buf = jnp.zeros((n_blocks * MOE_BLOCK,), jnp.float32).at[dest].set(w_sorted)
    blk_expert = jnp.minimum(jnp.searchsorted(pends, jnp.arange(n_blocks) * MOE_BLOCK, side='right'),
                             N_EXPERTS - 1)

    def run_block(args):
        toks, e = args
        a, g = jnp.split(h[toks] @ w_up[e], 2, axis=-1)
        return (jax.nn.silu(a) * g) @ w_down[e]

    y = lax.map(run_block, (tok_buf.reshape(n_blocks, MOE_BLOCK), blk_expert))
    y = y.reshape(-1, d) * w_buf[:, None].astype(h.dtype)
    return jnp.zeros_like(h).at[tok_buf].add(y)

def finish_layer(x, o_nsa, o_dil, merge, w_br_nsa, w_br_dil, w_out, norm_ffn, rg_w, rg_b, re_w, re_b, w_up, w_down):
    mix = (merge[..., 0, :] * (o_nsa @ w_br_nsa) + merge[..., 1, :] * (o_dil @ w_br_dil)) @ w_out
    x = x + mix
    b, t, d = x.shape
    h = rms_norm(x, norm_ffn).reshape(b * t, d)
    return x + hier_moe(h, rg_w, rg_b, re_w, re_b, w_up, w_down).reshape(b, t, d)

def setup_inputs(seed: int = 0) -> dict:
    key = jax.random.key(seed)
    ks = jax.random.split(key, 27)
    f32 = jnp.float32

    def nrm(k, shape, scale=1.0):
        return jax.random.normal(k, shape, f32) * scale

    n_pages = PAST_LEN // PAGE_SIZE
    n_pool = (5 * DEC_BATCH * n_pages + 3) // 4
    page_table = jax.random.permutation(ks[7], n_pool)[:DEC_BATCH * n_pages]
    page_table = page_table.reshape(DEC_BATCH, n_pages).astype(jnp.int32)
    return {
        'x_prompt': nrm(ks[0], (BATCH, SEQ, D_MODEL)),
        'x_sample': nrm(ks[1], (DEC_BATCH, DEC_SEQ, D_MODEL)),
        'cache_nsa_paged': nrm(ks[2], (DEPTH, n_pool, PAGE_SIZE, 4, NSA_KV_HEADS, HEAD_DIM)),
        'cache_nsa_win': nrm(ks[3], (DEPTH, DEC_BATCH, min(NSA_WINDOW, PAST_LEN), 2, NSA_KV_HEADS, HEAD_DIM)),
        'cache_dil_w128': nrm(ks[4], (DEPTH, DEC_BATCH, min(DIL_CONFIGS[0][0], PAST_LEN), 2, DIL_HEADS, HEAD_DIM)),
        'cache_dil_w512': nrm(ks[5], (DEPTH, DEC_BATCH, min(DIL_CONFIGS[1][0], PAST_LEN), 2, DIL_HEADS, HEAD_DIM)),
        'cache_dil_w2048': nrm(ks[6], (DEPTH, DEC_BATCH, min(DIL_CONFIGS[2][0], PAST_LEN), 2, DIL_HEADS, HEAD_DIM)),
        'page_table': page_table,
        'norm_mix': 1.0 + nrm(ks[8], (DEPTH, D_MODEL), 0.02),
        'w_in': nrm(ks[9], (DEPTH, D_MODEL, IN_DIM), D_MODEL ** -0.5),
        'cmp_pe_k': nrm(ks[10], (DEPTH, CMP_BLOCK, HEAD_DIM), 0.1),
        'cmp_w1_k': nrm(ks[11], (DEPTH, CMP_BLOCK * HEAD_DIM, CMP_HIDDEN), (CMP_BLOCK * HEAD_DIM) ** -0.5),
        'cmp_w2_k': nrm(ks[12], (DEPTH, CMP_HIDDEN, HEAD_DIM), CMP_HIDDEN ** -0.5),
        'cmp_pe_v': nrm(ks[13], (DEPTH, CMP_BLOCK, HEAD_DIM), 0.1),
        'cmp_w1_v': nrm(ks[14], (DEPTH, CMP_BLOCK * HEAD_DIM, CMP_HIDDEN), (CMP_BLOCK * HEAD_DIM) ** -0.5),
        'cmp_w2_v': nrm(ks[15], (DEPTH, CMP_HIDDEN, HEAD_DIM), CMP_HIDDEN ** -0.5),
        'w_branch_nsa': nrm(ks[16], (DEPTH, NSA_Q_DIM, D_MODEL), NSA_Q_DIM ** -0.5),
        'w_branch_dil': nrm(ks[17], (DEPTH, DIL_DIM, D_MODEL), DIL_DIM ** -0.5),
        'w_out': nrm(ks[18], (DEPTH, D_MODEL, D_MODEL), D_MODEL ** -0.5),
        'norm_ffn': 1.0 + nrm(ks[19], (DEPTH, D_MODEL), 0.02),
        'router_grp_w': nrm(ks[20], (DEPTH, D_MODEL, N_GROUPS), D_MODEL ** -0.5),
        'router_grp_b': nrm(ks[21], (DEPTH, N_GROUPS), 0.01),
        'router_exp_w': nrm(ks[22], (DEPTH, D_MODEL, N_EXPERTS), D_MODEL ** -0.5),
        'router_exp_b': nrm(ks[23], (DEPTH, N_EXPERTS), 0.01),
        'expert_w_up': nrm(ks[24], (DEPTH, N_EXPERTS, D_MODEL, 2 * EXPERT_FF), D_MODEL ** -0.5),
        'expert_w_down': nrm(ks[25], (DEPTH, N_EXPERTS, EXPERT_FF, D_MODEL), EXPERT_FF ** -0.5),
        'norm_final': 1.0 + nrm(ks[26], (D_MODEL,), 0.02),
    }

def reference(x_prompt, x_sample, cache_nsa_paged, cache_nsa_win, cache_dil_w128, cache_dil_w512,
              cache_dil_w2048, page_table, norm_mix, w_in, cmp_pe_k, cmp_w1_k, cmp_w2_k, cmp_pe_v, cmp_w1_v,
              cmp_w2_v, w_branch_nsa, w_branch_dil, w_out, norm_ffn, router_grp_w, router_grp_b, router_exp_w,
              router_exp_b, expert_w_up, expert_w_down, norm_final):
    b_p, t_p, _ = x_prompt.shape
    b_s, t_s, _ = x_sample.shape
    past_len = page_table.shape[1] * PAGE_SIZE
    pos_p = jnp.arange(t_p, dtype=jnp.int32)
    pos_s = past_len + jnp.arange(t_s, dtype=jnp.int32)
    dil_caches = (cache_dil_w128, cache_dil_w512, cache_dil_w2048)
    xp, xs = x_prompt, x_sample
    rows_p, rows_s, win_p, win_s = [], [], [], []
    dil_p = [[] for _ in range(N_DIL)]
    dil_s = [[] for _ in range(N_DIL)]
    for l in range(DEPTH):
        cmp_w = (cmp_pe_k[l], cmp_w1_k[l], cmp_w2_k[l], cmp_pe_v[l], cmp_w1_v[l], cmp_w2_v[l])
        tail_w = (w_branch_nsa[l], w_branch_dil[l], w_out[l], norm_ffn[l], router_grp_w[l], router_grp_b[l],
                  router_exp_w[l], router_exp_b[l], expert_w_up[l], expert_w_down[l])

        nsa, dil, merge = project_mixer_inputs(rms_norm(xp, norm_mix[l]), pos_p, w_in[l])
        q_rot, q_raw, k_c, v_c, k_s, v_s, k_w, v_w, g_nsa = nsa
        ctx = nsa_context(k_c, v_c, k_s, v_s, cmp_w)
        o_nsa = nsa_prompt(q_rot, q_raw, ctx, k_w, v_w, g_nsa)
        rows_p.append(jnp.stack([k_c, v_c, k_s, v_s], axis=2))
        win_p.append(jnp.stack([k_w, v_w], axis=2)[:, -min(NSA_WINDOW, t_p):])
        outs, lses = [], []
        for g in range(N_DIL):
            window, dil_rate = DIL_CONFIGS[g]
            q, k, v = dil[g]
            o, lse = dilated_prompt(q, k, v, window, dil_rate)
            outs.append(o)
            lses.append(lse)
            dil_p[g].append(jnp.stack([k, v], axis=2)[:, -min(window, t_p):])
        xp = finish_layer(xp, o_nsa, combine_dilations(outs, lses), merge, *tail_w)

        nsa, dil, merge = project_mixer_inputs(rms_norm(xs, norm_mix[l]), pos_s, w_in[l])
        q_rot, q_raw, k_c, v_c, k_s, v_s, k_w, v_w, g_nsa = nsa
        past = cache_nsa_paged[l][page_table].reshape(b_s, past_len, 4, NSA_KV_HEADS, HEAD_DIM)
        new_rows = jnp.stack([k_c, v_c, k_s, v_s], axis=2)
        rows = jnp.concatenate([past, new_rows], axis=1)
        ctx = nsa_context(rows[:, :, 0], rows[:, :, 1], rows[:, :, 2], rows[:, :, 3], cmp_w)
        n_w = cache_nsa_win.shape[2]
        win_all = jnp.concatenate([cache_nsa_win[l], jnp.stack([k_w, v_w], axis=2)], axis=1)
        win_pos = past_len - n_w + jnp.arange(n_w + t_s, dtype=jnp.int32)
        o_nsa = nsa_attend(q_rot, q_raw, pos_s, *ctx, win_all[:, :, 0], win_all[:, :, 1], win_pos, g_nsa)
        rows_s.append(new_rows)
        win_s.append(win_all[:, -n_w:])
        outs, lses = [], []
        for g in range(N_DIL):
            window, dil_rate = DIL_CONFIGS[g]
            q, k, v = dil[g]
            n_buf = dil_caches[g].shape[2]
            buf = jnp.concatenate([dil_caches[g][l], jnp.stack([k, v], axis=2)], axis=1)
            o, lse = dilated_sample(q, buf[:, :, 0], buf[:, :, 1], n_buf, window, dil_rate)
            outs.append(o)
            lses.append(lse)
            dil_s[g].append(buf[:, -n_buf:])
        xs = finish_layer(xs, o_nsa, combine_dilations(outs, lses), merge, *tail_w)

    y_prompt = rms_norm(xp, norm_final)
    y_sample = rms_norm(xs, norm_final)
    nsa_rows_prompt = jnp.stack(rows_p, axis=0)
    nsa_rows_sample = jnp.stack(rows_s, axis=0)
    nsa_win_prompt = jnp.stack(win_p, axis=0)
    nsa_win_sample = jnp.stack(win_s, axis=0)
    dil128_prompt = jnp.stack(dil_p[0], axis=0)
    dil128_sample = jnp.stack(dil_s[0], axis=0)
    dil512_prompt = jnp.stack(dil_p[1], axis=0)
    dil512_sample = jnp.stack(dil_s[1], axis=0)
    dil2048_prompt = jnp.stack(dil_p[2], axis=0)
    dil2048_sample = jnp.stack(dil_s[2], axis=0)
    return (y_prompt, y_sample, nsa_rows_prompt, nsa_rows_sample, nsa_win_prompt, nsa_win_sample,
            dil128_prompt, dil128_sample, dil512_prompt, dil512_sample, dil2048_prompt, dil2048_sample)


_drawn_inputs = setup_inputs


def setup_inputs(seed=0):
    import zlib

    import numpy as np

    out = dict(_drawn_inputs(seed))
    spreads = {}
    factors = {'norm_mix': 2.965,
     'cmp_pe_k': 6.553,
     'router_grp_b': 27.291,
     'router_exp_b': 4.946,
     'norm_final': 7.744,
     'cmp_pe_v': 4.357,
     'norm_ffn': 3.41}
    for name, (base, spread) in spreads.items():
        noise = np.random.default_rng([zlib.crc32(name.encode()), seed]).standard_normal(out[name].shape)
        drawn = base * np.exp(spread * noise) if base else spread * noise
        out[name] = __import__('jax').numpy.asarray(drawn.astype(out[name].dtype))
    for name, factor in factors.items():
        out[name] = (out[name] * factor).astype(out[name].dtype)
    return out
```

```python
import concourse.bass as bass
from concourse import mybir
from contextlib import ExitStack
import numpy as np

F32, I32, BF16 = mybir.dt.float32, mybir.dt.int32, mybir.dt.bfloat16
ALU, ACT, AX = mybir.AluOpType, mybir.ActivationFunctionType, mybir.AxisListType

P = 128
D = 1024
KD = D // P
TP, BS, SS = 512, 8, 4
TS = BS * SS
T = TP + TS
NT = TP // P
ROWS = [P] * NT + [TS]
HD, NH, KVH, REP = 64, 8, 2, 4
DH = 4
PAST, PAGE, NPAGE = 2048, 128, 16
STRIDE, CBLK = 16, 32
NCH = PAST // STRIDE
NCH_P = TP // STRIDE
QD, KVD, GD, DD = NH * HD, KVH * HD, 3 * NH, DH * HD
C_KV = QD
C_GATE = QD + 6 * KVD
C_DIL = C_GATE + GD
C_MRG = C_DIL + 9 * DD
C_KC, C_VC, C_KS, C_VS, C_KW, C_VW = (C_KV + i * KVD for i in range(6))
WCH = C_MRG // 11
WINDOWS = (128, 512, 2048)
HALF = 8
EPS = 1e-6
NEG = -1e30
FLOOR = -1e29
NG, EPG, NE, FF = 4, 8, 32, 256
BLK = 64
MINTURNS = (2 * T // BLK + 1) // 2
MAXTURNS = (NE + (2 * T - NE) // BLK + 1) // 2
MAXBLK = 2 * MAXTURNS
SLOTS = -(-(2 * T + 2 * BLK) // P) * P
SCALE = HD ** -0.5

MASK_AT = {"causal": (0, P), "dil0": (P, 2 * P), "dil1": (3 * P, NT * P), "dil2": (7 * P, NT * P), "cmp": (11 * P, NT * 32)}
MASKS_WIDTH = 12 * P

K_AT, _c = {}, 0
for _name, _n in (("hm", NH), ("hm_d", DH), ("row_tok", 16), ("row_tok_d", 16), ("esel", 2 * P), ("esel_d", 2 * P),
                  ("row_group", P), ("jmask", SS * P), ("new_mask", 2 * TS), ("dil_mask", 2 * 480), ("win_mask", 4),
                  ("before", 900), ("chunk_in_page", 1)):
    K_AT[_name] = (_c, _n)
    _c += _n
K_WIDTH = _c

R_AT, _c = {}, 0
for _name, _n in (("g_order", NG), ("e_order", EPG), ("is_token", NT + 1), ("token_id", NT + 1), ("ones", P), ("earlier", P),
                  ("e_before", NE * NE), ("block_no", MAXBLK), ("e_no", NE)):
    R_AT[_name] = (_c, _n)
    _c += _n
R_WIDTH = _c


def col_q(g):
    return C_DIL + g * 3 * DD


CREDIT = 1


class Link:

    def __init__(self, eng, sem, base=None):
        self.eng, self.sem, self.base, self.n = eng, sem, base, 0

    def __call__(self, ins):
        self.n += 1
        ins.then_inc(self.sem, 1)
        if self.base is None:
            self.eng.wait_ge(self.sem, self.n)
        else:
            self.eng.wait_ge(self.sem, self.base + self.n + CREDIT)


F32R = mybir.dt.float32r
UPPER = -4096


def upper_part(dve, out, src):
    return dve.tensor_copy(out, src)


def rest_part(dve, out, whole, upper):
    return dve.tensor_tensor(out, whole, upper, ALU.subtract)


def product_of_parts(pe, out, lhsT, rhs, first, last):
    a, b = lhsT, rhs
    pe.matmul(out, a[0], b[0], start=first, stop=False)
    pe.matmul(out, a[0], b[1], start=False, stop=False)
    return pe.matmul(out, a[1], b[0], start=False, stop=last)


def bc(ap, axis, shape):
    return ap.unsqueeze(axis).to_broadcast(shape)


class Program:
    def __init__(self, nc, ins, consts, outs, ctx):
        self.nc, self.i, self.c, self.o, self.ctx = nc, ins, consts, outs, ctx
        self.uncredited = []
        self.used = []

    def sb(self, ctx, name, shape, dt=F32):
        return ctx.enter_context(self.nc.sbuf_tensor(name, shape, dt))

    def parts_place(self, name, shape):
        return self.nc.alloc_sbuf_tensor_at(name, shape, F32R, offset=-(-self.nc.sbuf_base // 32) * 32)

    def ps(self, ctx, name, shape):
        return ctx.enter_context(self.nc.psum_tensor(name, shape, F32))

    def sem(self, name):
        self.used.append(self.nc.alloc_semaphore(name=name))
        return self.used[-1]

    def clear_semaphores(self):
        self.nc.clear_and_free_semaphores(self.used)
        self.used = []
        with self.nc.Block() as block:
            @block.sync
            def _(sp):
                sp.nop()

    def lsem(self, name):
        self.uncredited.append(self.sem(name))
        return self.uncredited[-1]

    def credit(self):
        with self.nc.Block() as block:
            @block.sync
            def _(sp):
                for s in self.uncredited:
                    sp.sem_inc(s, CREDIT)
        self.uncredited = []

    def norm_transpose(self, tag, xt, h, sq, gain, s_x, s_gain, hT, h_store=None, on_sync=None, on_pool=None,
                       beside_pe=None, beside_dve=None, split=None):
        nc = self.nc
        with ExitStack() as s:
            ms = self.sb(s, f"{tag}_ms", [P, 2 * (NT + 1)])
            tp = self.ps(s, f"{tag}_tp", [P, 4, 4, P])
            bp = self.ps(s, f"{tag}_beside_ps", [P, 512]) if beside_pe else None
            s_sq = self.sem(f"{tag}_squares_summed")
            s_h = self.sem(f"{tag}_h_ready")
            s_tp = self.sem(f"{tag}_transposed")
            s_ev = self.sem(f"{tag}_hT_written")
            s_rms = self.sem(f"{tag}_rms_ready")
            s_dve = self.sem(f"{tag}_dve_chain")
            s_st = self.sem(f"{tag}_h_stored")
            with nc.Block() as block:
                @block.sync
                def _(sp):
                    if on_sync is not None:
                        on_sync(sp)
                    if split is not None:
                        _, whole, dram, stored = split
                        for t in range(NT + 1):
                            sp.wait_ge(s_ev, 2 * t + 2)
                            sp.dma_start(dram[:, :, t * P:t * P + ROWS[t]], whole(t)).then_inc(stored, 16)
                    if h_store is not None:
                        for t in range(NT + 1):
                            sp.wait_ge(s_h, t + 1)
                            sp.dma_start(h_store[t * P:t * P + ROWS[t], :], h[:ROWS[t], t, :]).then_inc(s_st, 16)
                        sp.wait_ge(s_st, 16 * (NT + 1))

                @block.scalar
                def _(act):
                    for t in range(NT + 1):
                        if s_x is not None:
                            act.wait_ge(s_x[t], 16)
                        if t > 0:
                            act.wait_ge(s_sq, t)
                        act.activation(sq[:ROWS[t], :], xt[:ROWS[t], t, :], ACT.Square,
                                       accum_out=ms[:ROWS[t], t:t + 1]).then_inc(s_sq, 1)
                        act.wait_ge(s_sq, t + 1)
                        act.activation(ms[:ROWS[t], t:t + 1], ms[:ROWS[t], t:t + 1], ACT.Sqrt,
                                       bias=self.eps[:ROWS[t], :], scale=1.0 / D).then_inc(s_rms, 1)
                    if split is not None:
                        for t in range(NT + 1):
                            for half in range(2):
                                act.wait_ge(s_tp, 2 * t + half + 1)
                                act.copy(split[1](t)[:, 4 * half:4 * half + 4, :],
                                         tp[:, 2 * (t % 2) + half, :, :ROWS[t]]).then_inc(s_ev, 1)

                @block.gpsimd
                def _(pool):
                    if on_pool is not None:
                        on_pool(pool)

                def evacuate(dve, link, t):
                    n = ROWS[t]
                    if split is not None:
                        rest, whole, _, _ = split
                        whole = whole(t)
                        dve.wait_ge(s_ev, 2 * t + 2)
                        link(upper_part(dve, hT[:, :, t * P:t * P + n], whole))
                        rest_part(dve, rest[:, :, t * P:t * P + n], whole, hT[:, :, t * P:t * P + n])
                        return
                    for half in range(2):
                        dve.wait_ge(s_tp, 2 * t + half + 1)
                        dve.tensor_copy(hT[:, 4 * half:4 * half + 4, t * P:t * P + n],
                                        tp[:, 2 * (t % 2) + half, :, :n]).then_inc(s_ev, 1)

                @block.vector
                def _(dve):
                    link = Link(dve, s_dve)
                    if beside_dve is not None:
                        beside_dve[0](dve, bp)
                    dve.wait_ge(s_gain, 16)
                    for t in range(NT + 1):
                        n = ROWS[t]
                        dve.wait_ge(s_rms, t + 1)
                        inv = ms[:n, NT + 1 + t:NT + 2 + t]
                        link(dve.reciprocal(inv, ms[:n, t:t + 1]))
                        dve.scalar_tensor_tensor(h[:n, t, :], xt[:n, t, :], inv, gain[:n, :],
                                                 ALU.mult, ALU.mult).then_inc(s_h, 1)
                        if t > 0:
                            evacuate(dve, link, t - 1)
                    evacuate(dve, link, NT)
                    if beside_dve is not None:
                        beside_dve[1](dve, bp)

                @block.tensor
                def _(pe):
                    if beside_pe is not None:
                        beside_pe(pe, bp)
                    for t in range(NT + 1):
                        n = ROWS[t]
                        pe.wait_ge(s_h, t + 1)
                        if t >= 2:
                            pe.wait_ge(s_ev, 2 * t - 2)
                        for k in range(KD):
                            ins = pe.transpose(tp[:, 2 * (t % 2) + k // 4, k % 4, :n],
                                               h[:n, t, k * P:(k + 1) * P], self.ident[:n, :n])
                            if k % 4 == 3:
                                ins.then_inc(s_tp, 1)

    def project(self, hT, hT_rest, w, wu, wr, s_w, rows, src, s_saved, tables_loaded):
        nc = self.nc
        w_in = self.i["w_in"][0]
        TURNS = C_MRG // WCH // 2
        KV_TURNS = -(-(C_KC + 4 * HD) // (2 * WCH))
        with ExitStack() as s:
            acc = self.ps(s, "proj_acc", [P, 8, 512])
            s_up = self.lsem("w_in_upper_ready")
            s_sp = self.lsem("w_in_split")
            s_mm = [self.lsem(f"proj_accumulated{u}") for u in range(2)]
            s_act = self.lsem("proj_copied_by_act")
            s_dve = self.lsem("proj_copied_by_dve")
            s_src = self.lsem("compressor_source_copied")
            self.credit()
            with nc.Block() as block:
                @block.sync
                def _(sp):
                    def load(u, k):
                        sp.wait_ge(s_mm[u], (NT + 1) * k + CREDIT)
                        sp.dma_start(w[:, u, :, :], w_in[:, bass.ds((2 * k + u) * WCH, WCH)]
                                     .rearrange("(k p) c -> p k c", p=P)).then_inc(s_w[u], 16)

                    with sp.Fori(0, TURNS - 1) as i:
                        load(0, i + 1)
                        load(1, i + 1)
                    load(0, TURNS)
                    sp.wait_ge(s_act, 5 * KV_TURNS + CREDIT)
                    sp.wait_ge(s_dve, 5 * KV_TURNS + CREDIT)
                    for t in range(NT):
                        for kg in range(4):
                            c = C_KC + kg * HD
                            sp.dma_start(src[8 * t:8 * t + 8, kg], rows[:, t, c:c + HD]).then_inc(s_src, 16)
                    sp.wait_ge(s_src, 16 * 4 * NT + CREDIT)
                    tables_loaded(sp)

                @block.tensor
                def _(pe):
                    def chunk(u, k):
                        pe.wait_ge(s_sp, 2 * k + u + 1 + CREDIT)
                        if u == 0:
                            pe.wait_ge(s_act, 5 * k + CREDIT)
                            pe.wait_ge(s_dve, 5 * k + CREDIT)
                        for t in range(NT + 1):
                            n = 5 * u + t
                            if n >= 8:
                                pe.wait_ge((s_act, s_dve)[(n - 8) % 2], 5 * k + (n - 8) // 2 + 1 + CREDIT)
                            tok = slice(t * P, t * P + ROWS[t])
                            for c in range(KD):
                                ins = product_of_parts(pe, acc[:ROWS[t], n % 8, 0:WCH],
                                                       (hT[:, c, tok], hT_rest[:, c, tok]),
                                                       (wu[:, u, c, :], wr[:, u, c, :]), c == 0, c == KD - 1)
                            ins.then_inc(s_mm[u], 1)

                    with pe.Fori(0, TURNS) as i:
                        chunk(0, i)
                        chunk(1, i)
                    chunk(0, TURNS)

                def copies(eng, which, copy, done, u, k):
                    for t in range(NT + 1):
                        n = 5 * u + t
                        if n % 2 == which:
                            eng.wait_ge(s_mm[u], (NT + 1) * k + t + 1 + CREDIT)
                            copy(rows[:ROWS[t], t, bass.ds((2 * k + u) * WCH, WCH)],
                                 acc[:ROWS[t], n % 8, 0:WCH]).then_inc(done, 1)

                @block.scalar
                def _(act):
                    act.wait_ge(s_saved, 16 * (NT + 1))
                    with act.Fori(0, TURNS) as i:
                        for u in range(2):
                            copies(act, 0, act.copy, s_act, u, i)
                    copies(act, 0, act.copy, s_act, 0, TURNS)

                @block.vector
                def _(dve):
                    def split(u, k):
                        dve.wait_ge(s_w[u], 16 * k + 16 + CREDIT)
                        upper_part(dve, wu[:, u], w[:, u]).then_inc(s_up, 1)
                        dve.wait_ge(s_up, 2 * k + u + 1 + CREDIT)
                        rest_part(dve, wr[:, u], w[:, u], wu[:, u]).then_inc(s_sp, 1)

                    split(0, 0)
                    dve.wait_ge(s_saved, 16 * (NT + 1))
                    with dve.Fori(0, TURNS) as i:
                        split(1, i)
                        copies(dve, 1, dve.tensor_copy, s_dve, 0, i)
                        split(0, i + 1)
                        copies(dve, 1, dve.tensor_copy, s_dve, 1, i)
                    copies(dve, 1, dve.tensor_copy, s_dve, 0, TURNS)

    def finish_rows(self, rows, qrot, src, kcT, vc):
        nc = self.nc
        o = self.o
        n = NCH_P
        with ExitStack() as s:
            ra = self.sb(s, "rot_products", [P, 2, 4, 3 * 8 * HALF])
            tp = [self.ps(s, f"pc_tp{j}", [P, 512]) for j in range(2)]
            hp = [self.ps(s, f"pc_hp{j}", [P, 512]) for j in range(2)]
            kp = self.ps(s, "pc_kp", [P, 512])
            b = self.compress_buffers(s, "pc", n, tp, hp, kp, self.lsem("pc_transposed"),
                                      [self.lsem("pc_xT_by_dve"), self.lsem("pc_xT_by_act")])
            s_qc = self.lsem("q_copied")
            s_gt = self.lsem("gates_ready")
            s_rot = [self.lsem(f"rows_rotated_by_{e}") for e in ("pool", "dve")]
            s_rc = [self.lsem(f"rot_chain_of_{e}") for e in ("pool", "dve")]
            self.credit()
            with nc.Block() as block:
                @block.sync
                def _(sp):
                    sp.wait_ge(s_gt, NT + 1 + CREDIT)

                    def put(dst, src):
                        self.n_rows_out += 1
                        sp.dma_start(dst, src).then_inc(self.s_rows_out, 16)

                    for t in range(NT + 1):
                        sp.wait_ge(s_rot[0], 2 * (t + 1) + CREDIT)
                        sp.wait_ge(s_rot[1], t + 1 + CREDIT)
                        if t < NT:
                            tok = slice(t * P, (t + 1) * P)
                            put(o["nsa_rows_prompt"][0, 0, tok].rearrange("t c g d -> t (c g d)"),
                                rows[:, t, C_KC:C_KW])
                            put(o["nsa_win_prompt"][0, 0, tok].rearrange("t c g d -> t (c g d)"),
                                rows[:, t, C_KW:C_GATE])
                            for g in range(3):
                                wlen = min(WINDOWS[g], TP)
                                lo = t * P - (TP - wlen)
                                if lo >= 0:
                                    put(o[f"dil{WINDOWS[g]}_prompt"][0, 0, lo:lo + P].rearrange("t c g d -> t (c g d)"),
                                        rows[:, t, col_q(g) + DD:col_q(g) + 3 * DD])
                        else:
                            put(o["nsa_rows_sample"][0].rearrange("b s c g d -> (b s) (c g d)"),
                                rows[:TS, t, C_KC:C_KW])
                            put(o["nsa_win_sample"][0][:, 512 - SS:512].rearrange("b s c g d -> b s (c g d)"),
                                rows[:TS, t, C_KW:C_GATE])
                            for g in range(3):
                                w = WINDOWS[g]
                                put(o[f"dil{w}_sample"][0][:, w - SS:w].rearrange("b s c g d -> b s (c g d)"),
                                    rows[:TS, t, col_q(g) + DD:col_q(g) + 3 * DD])

                @block.tensor
                def _(pe):
                    self.compress_pe(pe, b, lambda kg, j: src[:, kg, 2 * j:2 * j + 2, :].rearrange("c a d -> c (a d)"), 0,
                                     lambda kg: None)

                @block.scalar
                def _(act):
                    for t in range(NT + 1):
                        act.copy(qrot[:ROWS[t], t, :], rows[:ROWS[t], t, 0:QD]).then_inc(s_qc, 1)
                    for t in range(NT + 1):
                        g = rows[:ROWS[t], t, C_GATE:C_DIL]
                        act.activation(g, g, ACT.Sigmoid).then_inc(s_gt, 1)
                    self.compress_act(act, b, 0)

                def rotate(eng, which, n, t, r):
                    m, a, hh = r.shape[0], r.shape[1], r.shape[2]
                    sh = [m, a, hh, HALF]
                    if n > 0:
                        eng.wait_ge(s_rot[which], n + CREDIT)
                        eng.nop(nofuse=True)
                    x1, x2 = r[:, :, :, 0:HALF], r[:, :, :, HALF:2 * HALF]
                    tmp = [ra[:m, which, j, 0:a * hh * HALF].rearrange("p (a h d) -> p a h d", a=a, h=hh)
                           for j in range(4)]
                    cos = bc(bc(self.cs[:m, t, 0, :], 1, [m, hh, HALF]), 1, sh)
                    sin = bc(bc(self.cs[:m, t, 1, :], 1, [m, hh, HALF]), 1, sh)
                    eng.tensor_tensor(tmp[0], x1, cos, ALU.mult)
                    eng.tensor_tensor(tmp[1], x2, sin, ALU.mult)
                    eng.tensor_tensor(tmp[2], x2, cos, ALU.mult)
                    eng.tensor_tensor(tmp[3], x1, sin, ALU.mult).then_inc(s_rc[which], 1)
                    eng.wait_ge(s_rc[which], n + 1 + CREDIT)
                    eng.nop(nofuse=True)
                    eng.tensor_tensor(x1, tmp[0], tmp[1], ALU.subtract)
                    eng.tensor_tensor(x2, tmp[2], tmp[3], ALU.add).then_inc(s_rot[which], 1)

                @block.vector
                def _(dve):
                    for t in range(NT + 1):
                        rotate(dve, 1, t, t, rows[:ROWS[t], t, C_DIL:C_MRG].rearrange(
                            "p (a h d) -> p a h d", a=3, d=HD)[:, :, 0:2 * DH])
                        if t == 0:
                            self.compress_dve(dve, b, 0, kcT, vc)

                @block.gpsimd
                def _(pool):
                    for t in range(NT + 1):
                        m = ROWS[t]
                        rotate(pool, 0, 2 * t, t, rows[:m, t, C_KS:C_KS + 4 * KVD].rearrange(
                            "p (a x h d) -> p a x h d", a=2, x=2, d=HD)[:, :, 0])
                        pool.wait_ge(s_qc, t + 1 + CREDIT)
                        pool.nop(nofuse=True)
                        rotate(pool, 0, 2 * t + 1, t, qrot[:m, t, :].rearrange("p (a h d) -> p a h d", a=1, d=HD))

    def move_cache(self, sp, src, dst, b):
        src, dst = self.i[src][0], self.o[dst][0]
        w, row = src.shape[1], int(np.prod(src.shape[2:]))
        n = (w - SS) * row
        y = max(d for d in range(1, 1025) if n % (P * d) == 0) if n % P == 0 else n // 16
        flat = "b w c h d -> b (w c h d)"
        sp.dma_start(dst.rearrange(flat)[bass.ds(b, 1), 0:n].rearrange("b (x y) -> (b x) y", y=y),
                     src.rearrange(flat)[bass.ds(b, 1), SS * row:w * row].rearrange("b (x y) -> (b x) y", y=y)
                     ).then_inc(self.s_moved, 16)

    def first_loads(self, rows, gain, w):
        nc = self.nc
        w_in = self.i["w_in"][0]
        s_w = [self.lsem(f"w_in_loaded{u}") for u in range(2)]
        s_x = [self.sem(f"x_loaded{t}") for t in range(NT + 1)]
        s_id, s_gain, s_eps = self.sem("identity_loaded"), self.sem("gain_loaded"), self.sem("eps_and_zeros_ready")
        s_cmp, s_m, s_c = self.sem("cmp_w_loaded"), self.sem("masks_loaded"), self.sem("tables_loaded")
        s_cast = self.sem("masks_cast")
        self.s_pages = self.sem("page_table_loaded")
        self.credit()
        with nc.Block() as block:
            @block.sync
            def _(sp):
                sp.dma_start(self.ident[:, :], self.c["ident"]).then_inc(s_id, 16)
                for kv, name in enumerate("kv"):
                    sp.dma_start(self.pe_rows[:, kv, :], self.i[f"cmp_pe_{name}"][0].rearrange("(j a) d -> j (a d)", a=2)).then_inc(s_cmp, 16)
                    sp.dma_start(self.w1[:, kv], self.i[f"cmp_w1_{name}"][0].rearrange("(j p) h -> p j h", p=P)).then_inc(s_cmp, 16)
                for t in range(NT + 1):
                    sp.dma_start(rows[:ROWS[t], t, 0:D], self.x_src[t]).then_inc(s_x[t], 16)
                sp.dma_start(gain, self.i["norm_mix"][0].partition_broadcast(P)).then_inc(s_gain, 16)
                sp.wait_ge(s_id, 16)

            @block.vector
            def _(dve):
                dve.memset(self.eps[:, :], EPS).then_inc(s_eps, 1)
                dve.memset(self.w2k[:, :, :], 0.0).then_inc(s_eps, 1)

        def load_tables(sp):
            for u in range(2):
                sp.dma_start(w[:, u, :, :], w_in[:, u * WCH:(u + 1) * WCH].rearrange("(k p) c -> p k c", p=P)).then_inc(s_w[u], 16)
            sp.dma_start(self.cs[:, :, :, :], self.c["cos_sin"]).then_inc(s_c, 16)
            sp.dma_start(self.masks_f, self.c["masks"]).then_inc(s_m, 16)
            for c in range(8):
                sp.dma_start(self.page_rows[c:P:8, 0, :], self.i["page_table"].rearrange("b p -> p b"),
                             allow_slow_non_contiguous=True).then_inc(self.s_pages, 16)
            for g in range(2):
                sp.dma_start(self.w2k[:, g, g * HD:(g + 1) * HD], self.i["cmp_w2_k"][0]).then_inc(s_c, 16)
            sp.dma_start(self.w2v[:, :], self.i["cmp_w2_v"][0]).then_inc(s_c, 16)

        def tables_loaded(sp):
            sp.wait_ge(s_c, 4 * 16)

        s_bp, s_bd = self.sem("cmp_bias_by_pe"), self.sem("cmp_bias_by_dve")

        def bias_pe(pe, bp):
            pe.wait_ge(s_cmp, 4 * 16)
            for kv in range(2):
                ins = pe.transpose(bp[:, kv * 16:kv * 16 + 16], self.pe_rows[:, kv, :], self.ident[:16, :16])
            ins.then_inc(s_bp, 1)
            pe.wait_ge(s_bd, 1)
            for kv in range(2):
                for j in range(16):
                    ins = pe.matmul(bp[:, 64 + kv:65 + kv], self.w1[:, kv, j, :], self.peT[:, kv, j:j + 1],
                                    start=j == 0, stop=j == 15)
            ins.then_inc(s_bp, 1)

        def pe_copied(dve, bp):
            dve.wait_ge(s_bp, 1)
            dve.tensor_copy(self.peT[:, :, :], bp[:, 0:32].rearrange("p (a j) -> p a j", a=2)).then_inc(s_bd, 1)

        def bias_copied(dve, bp):
            dve.wait_ge(s_bp, 2)
            dve.tensor_copy(self.pe_bias[:, :], bp[:, 64:66]).then_inc(s_bd, 1)

        def cast_masks(pool):
            pool.wait_ge(s_m, 16)
            pool.tensor_copy(self.ident_b[:, :], self.ident[:, :]).then_inc(s_cast, 1)
            pool.tensor_copy(self.masks_b[:, :], self.masks_f).then_inc(s_cast, 1)

        beside = dict(on_sync=load_tables, on_pool=cast_masks, beside_pe=bias_pe, beside_dve=(pe_copied, bias_copied))
        return s_w, s_x, s_gain, beside, tables_loaded

    def k(self, name, parts=P):
        a, n = K_AT[name]
        return self.ks[:parts, a:a + n]

    def r(self, name):
        a, n = R_AT[name]
        return self.rs[:, a:a + n]

    def mask(self, name):
        a, n = MASK_AT[name]
        return self.masks_b[:, a:a + n]

    def compress_buffers(self, s, tag, n, tp, hp, kp, s_tp, s_ev, tp_per=8, ev_per=4):
        b = dict(n=n, tp=tp, hp=hp, kp=kp, s_tp=s_tp, s_ev=s_ev, tp_per=tp_per, ev_per=ev_per)
        b["xT"] = self.sb(s, f"{tag}_xT", [P, 2, 8, n])
        b["hid"] = self.sb(s, f"{tag}_hidden", [P, 4, n])
        b["s_h"] = [self.lsem(f"{tag}_hidden_summed{j}") for j in range(4)]
        b["s_g"] = self.lsem(f"{tag}_gelu_done")
        b["s_kv"] = self.lsem(f"{tag}_compressed")
        b["s_out"] = self.lsem(f"{tag}_compressed_copied")
        return b

    def compress_pe(self, pe, b, src, call, src_ready):
        n = b["n"]
        e0 = b["ev_per"] * call + b["ev_per"] - 4

        def transposes(kg):
            src_ready(kg)
            for half in range(2):
                pe.wait_ge(b["s_ev"][half], e0 + kg + CREDIT)
                for jj in range(4):
                    ins = pe.transpose(b["tp"][half][:, jj * n:(jj + 1) * n], src(kg, 4 * half + jj),
                                       self.ident[:n, :n])
                ins.then_inc(b["s_tp"], 1)

        def hidden(kg):
            pe.wait_ge(b["s_ev"][0], e0 + kg + 1 + CREDIT)
            pe.wait_ge(b["s_ev"][1], e0 + kg + 1 + CREDIT)
            pe.wait_ge(b["s_g"], 4 * call + max(kg - 1, 0) + CREDIT)
            for j in range(16):
                ins = pe.matmul(b["hp"][kg % 2][:, 0:n - 1], self.w1[:, kg // 2, j, :],
                                b["xT"][:, kg % 2, j % 8, j // 8:j // 8 + n - 1], start=j == 0, stop=j == 15)
            ins.then_inc(b["s_h"][kg], 1)

        transposes(0)
        for kg in range(4):
            if kg < 3:
                transposes(kg + 1)
            hidden(kg)
        pe.wait_ge(b["s_g"], 4 * call + 4 + CREDIT)
        pe.wait_ge(b["s_out"], 2 * call + CREDIT)
        for g in range(2):
            pe.matmul(b["kp"][:, 0:n - 1], self.w2k[:, g, :], b["hid"][:, g, 0:n - 1], start=g == 0, stop=g == 1)
        for g in range(2):
            ins = pe.matmul(b["kp"][0:n - 1, P + g * HD:P + (g + 1) * HD], b["hid"][:, 2 + g, 0:n - 1],
                            self.w2v[:, :], start=True, stop=True)
        ins.then_inc(b["s_kv"], 1)

    def compress_copies(self, eng, copy, b, half, kg, call):
        n = b["n"]
        if kg < 2:
            eng.wait_ge(b["s_h"][kg + 2], call + CREDIT)
        else:
            eng.wait_ge(b["s_h"][kg - 2], call + 1 + CREDIT)
        eng.wait_ge(b["s_tp"], b["tp_per"] * (call + 1) - 8 + 2 * kg + half + 1 + CREDIT)
        copy(b["xT"][:, kg % 2, 4 * half:4 * half + 4, :],
             b["tp"][half][:, 0:4 * n].rearrange("p (a c) -> p a c", a=4)).then_inc(b["s_ev"][half], 1)

    def compress_act(self, act, b, call):
        n = b["n"]

        def gelu(kg):
            act.wait_ge(b["s_h"][kg], call + 1 + CREDIT)
            if kg == 0:
                act.wait_ge(b["s_kv"], call + CREDIT)
            act.activation(b["hid"][:, kg, 0:n - 1], b["hp"][kg % 2][:, 0:n - 1],
                           ACT.Gelu_apprx_tanh, bias=self.pe_bias[:, kg // 2:kg // 2 + 1]).then_inc(b["s_g"], 1)

        self.compress_copies(act, act.copy, b, 1, 0, call)
        for kg in range(4):
            if kg < 3:
                self.compress_copies(act, act.copy, b, 1, kg + 1, call)
            gelu(kg)

    def compress_dve(self, dve, b, call, kT, v, beside=None):
        n = b["n"]
        for kg in range(4):
            self.compress_copies(dve, dve.tensor_copy, b, 0, kg, call)
            if beside is not None:
                beside(kg)
        dve.wait_ge(b["s_kv"], call + 1 + CREDIT)
        dve.tensor_copy(kT, b["kp"][:, 0:n - 1]).then_inc(b["s_out"], 1)
        dve.tensor_copy(v, b["kp"][0:n - 1, P:2 * P]).then_inc(b["s_out"], 1)

    def prompt_nsa(self, rows, qrot, kcT, vc, o_tok):
        nc = self.nc
        NC = NCH_P - 1
        U = KVH * NT
        with ExitStack() as s:
            kT = self.sb(s, "pn_kT", [P, 2, TP])
            stq = self.sb(s, "pn_q_staged", [P, 2, NT, P])
            qT = self.sb(s, "pn_qT", [P, 2, KVH, TP])
            ex = self.sb(s, "pn_exp", [P, 2, 2, TP])
            pT = self.sb(s, "pn_pT", [P, 2, TP])
            st = self.sb(s, "pn_stats", [P, 4, 4, 2])
            oa = self.sb(s, "pn_o_partial", [P, 2, HD])
            cx = self.sb(s, "pn_cmp_exp", [P, U, 32])
            cst = self.sb(s, "pn_cmp_stats", [P, 2, U])
            pcT = self.sb(s, "pn_cmp_pT", [P, KVH, P])
            vcz = self.sb(s, "pn_cmp_v_by_tile", [P, NT, KVD])
            S = [self.ps(s, f"pn_S{b}", [P, 2, 512]) for b in range(2)]
            O2 = self.ps(s, "pn_O", [P, 2, 512])
            O = [O2[:, b, :] for b in range(2)]
            PT = [self.ps(s, f"pn_PT{b}", [P, 512]) for b in range(2)]
            CS, CT = O2[:, :, 0:P], O2[:, :, 256:256 + P]
            s_kt = self.lsem("pn_k_transposed")
            s_kc = self.lsem("pn_kT_copied")
            s_z = self.lsem("pn_zeroed")
            s_vz = self.lsem("pn_cmp_v_placed")
            s_ks = self.lsem("sample_tables_loaded")
            s_st = self.lsem("pn_q_staged")
            s_qt = self.lsem("pn_q_transposed")
            s_qd = self.lsem("pn_qT_raw_copied")
            s_qa = self.lsem("pn_qT_rot_copied")
            s_cs = self.lsem("pn_cmp_scores_ready")
            s_cd = self.lsem("pn_cmp_differences_ready")
            s_ce = self.lsem("pn_cmp_exp_done")
            s_cp = self.lsem("pn_cmp_probs_ready")
            s_ct = self.lsem("pn_cmp_probs_transposed")
            s_cc = self.lsem("pn_cmp_pT_copied")
            s_s = self.lsem("pn_scores_ready")
            s_nm = self.lsem("pn_negmax_ready")
            s_ex = self.lsem("pn_exp_done")
            s_t = self.lsem("pn_probs_transposed")
            s_pd = self.lsem("pn_pT_sel_copied")
            s_pa = self.lsem("pn_pT_win_copied")
            s_pv = self.lsem("pn_pv_done")
            s_o = self.lsem("pn_o_written")
            s_dc = self.lsem("pn_dve_chain")
            LINKS = 5 * U + 6
            self.credit()
            with nc.Block() as block:
                @block.tensor
                def _(pe):
                    for j, c in enumerate((C_KS, C_KW)):
                        for t in range(NT):
                            ins = pe.transpose(PT[j][:, t * P:(t + 1) * P], rows[:, t, c:c + KVD], self.ident[:, :])
                        ins.then_inc(s_kt, 1)
                    pe.wait_ge(s_kc, 2 + CREDIT)
                    pe.wait_ge(s_vz, 16 * NT + CREDIT)
                    pe.wait_ge(s_z, 3 + CREDIT)
                    with pe.Fori(0, REP) as r:
                        pe.wait_ge(s_st, 2 * r + 2 + CREDIT)
                        pe.wait_ge(s_pd, U * r + CREDIT)
                        pe.wait_ge(s_pa, U * r + CREDIT)
                        for j in range(2):
                            for t in range(NT):
                                ins = pe.transpose(PT[j][:, t * P:(t + 1) * P], stq[:, j, t, :], self.ident[:, :])
                            ins.then_inc(s_qt, 1)

                        def scores(u):
                            g, i = divmod(u, NT)
                            bf = u % 2
                            n = (i + 1) * P
                            pe.wait_ge(s_ex, U * r + max(u - 1, 0) + CREDIT)
                            for j in range(2):
                                pe.matmul(S[bf][:, j, 0:n], qT[:, 1, g, i * P:(i + 1) * P],
                                          kT[:, j, 0:n], start=True, stop=False)
                                ins = pe.matmul(S[bf][:, j, n - P:n], self.ident_b[:, :], self.mask("causal"),
                                                start=False, stop=True)
                            ins.then_inc(s_s, 1)

                        def compressed_scores():
                            for g in range(KVH):
                                pe.matmul(CS[:, g, :], self.ident_b[:, :], self.mask("cmp"), start=True, stop=False)
                                for i in range(NT):
                                    ins = pe.matmul(CS[:, g, 32 * i:32 * i + NC], qT[:, 0, g, i * P:(i + 1) * P],
                                                    kcT[:, :], start=False, stop=i == NT - 1)
                            ins.then_inc(s_cs, 1)

                        def trans(u):
                            g, i = divmod(u, NT)
                            pe.wait_ge(s_ex, U * r + u + 1 + CREDIT)
                            for j, copied in enumerate((s_pd, s_pa)):
                                pe.wait_ge(copied, U * r + u + CREDIT)
                                for kb in range(i + 1):
                                    ins = pe.transpose(PT[j][:, kb * P:(kb + 1) * P],
                                                       ex[:, u % 2, j, kb * P:(kb + 1) * P], self.ident[:, :])
                                ins.then_inc(s_t, 1)

                        def pv(u):
                            g, i = divmod(u, NT)
                            pe.wait_ge(s_o, U * r + max(u - 1, 0) + CREDIT)
                            if u == 0:
                                pe.wait_ge(s_cc, r + 1 + CREDIT)
                            for j, (c, copied) in enumerate(((C_VS, s_pd), (C_VW, s_pa))):
                                pe.wait_ge(copied, U * r + u + 1 + CREDIT)
                                for kb in range(i + 1):
                                    pe.matmul(O[u % 2][:, j * P:(j + 1) * P], pT[:, j, kb * P:(kb + 1) * P],
                                              rows[:, kb, c:c + KVD], start=kb == 0, stop=kb == i)
                            pe.matmul(O[u % 2][:, 2 * P:3 * P], pcT[:, g, :], vcz[:, i, :],
                                      start=True, stop=True).then_inc(s_pv, 1)

                        pe.wait_ge(s_qa, r + 1 + CREDIT)
                        scores(0)
                        scores(1)
                        pe.wait_ge(s_qd, r + 1 + CREDIT)
                        pe.wait_ge(s_o, U * r + CREDIT)
                        compressed_scores()
                        trans(0)
                        pe.wait_ge(s_cp, r + 1 + CREDIT)
                        for g in range(KVH):
                            ins = pe.transpose(CT[:, g, :],
                                               cx[:, g * NT:(g + 1) * NT, :].rearrange("p u c -> p (u c)"), self.ident[:, :])
                        ins.then_inc(s_ct, 1)
                        for u in range(U):
                            if u + 2 < U:
                                scores(u + 2)
                            pv(u)
                            if u + 1 < U:
                                trans(u + 1)

                @block.sync
                def _(sp):
                    sp.dma_start(self.ks[:, :], self.c["sample"]).then_inc(s_ks, 16)
                    sp.wait_ge(s_z, 1 + CREDIT)
                    for i in range(NT):
                        sp.dma_start(vcz[32 * i:32 * i + NC, i, :], vc[:, :]).then_inc(s_vz, 16)
                    with sp.Fori(0, REP) as r:
                        sp.wait_ge(s_qt, 2 * r + 2 + CREDIT)
                        for j in range(BS // REP):
                            self.move_cache(sp, "cache_dil_w2048", "dil2048_sample", BS // REP * r + j)
                    sp.wait_ge(s_ks, 16 + CREDIT)

                @block.gpsimd
                def _(pool):
                    pool.memset(vcz[:, :, :], 0.0).then_inc(s_z, 1)
                    pool.memset(cx[:, :, :], 0.0).then_inc(s_z, 1)
                    pool.memset(qT[:, :, :, :], 0.0).then_inc(s_z, 1)
                    with pool.Fori(0, REP) as r:
                        pool.wait_ge(s_qt, 2 * r + CREDIT)
                        pool.nop(nofuse=True)
                        for j, src in ((1, qrot), (0, rows)):
                            q = src[:, 0:NT, 0:QD].rearrange("p t (g x) -> p t g x", g=KVH)[:, :, :, bass.ds(r * HD, HD)]
                            pool.tensor_copy(stq[:, j].rearrange("p t (g d) -> p t g d", g=KVH), q).then_inc(s_st, 1)

                @block.scalar
                def _(act):
                    act.wait_ge(s_kt, 2 + CREDIT)
                    act.copy(kT[:, 1, :], PT[1][:, :]).then_inc(s_kc, 1)
                    act.wait_ge(s_z, 3 + CREDIT)
                    with act.Fori(0, REP) as r:
                        act.wait_ge(s_qt, 2 * r + 2 + CREDIT)
                        act.copy(qT[0:HD, 1, 0, :], PT[1][0:HD, :])
                        act.copy(qT[HD:P, 1, 1, :], PT[1][HD:P, :]).then_inc(s_qa, 1)

                        def exps(u):
                            g, i = divmod(u, NT)
                            n = (i + 1) * P
                            act.wait_ge(s_nm, U * r + u + 1 + CREDIT)
                            act.wait_ge(s_t, 2 * U * r + 2 * max(u - 1, 0) + CREDIT)
                            for j in range(2):
                                ins = act.activation(ex[:, u % 2, j, 0:n], S[u % 2][:, j, 0:n], ACT.Exp,
                                                     bias=st[:, u % 4, 1, j:j + 1], scale=SCALE,
                                                     accum_out=st[:, u % 4, 2, j:j + 1])
                            ins.then_inc(s_ex, 1)

                        def copy_pT(u):
                            n = (u % NT + 1) * P
                            act.wait_ge(s_t, 2 * U * r + 2 * u + 2 + CREDIT)
                            act.copy(pT[:, 1, 0:n], PT[1][:, 0:n]).then_inc(s_pa, 1)

                        exps(0)
                        exps(1)
                        act.wait_ge(s_cd, r + 1 + CREDIT)
                        act.activation(cx[:, :, 0:NC], cx[:, :, 0:NC], ACT.Exp, scale=SCALE).then_inc(s_ce, 1)
                        copy_pT(0)
                        act.wait_ge(s_ct, r + 1 + CREDIT)
                        act.copy(pcT[:, :, :], CT).then_inc(s_cc, 1)
                        for u in range(U):
                            if u + 2 < U:
                                exps(u + 2)
                            if u + 1 < U:
                                copy_pT(u + 1)

                @block.vector
                def _(dve):
                    dve.wait_ge(s_kt, 1 + CREDIT)
                    dve.tensor_copy(kT[:, 0, :], PT[0][:, :]).then_inc(s_kc, 1)
                    dve.wait_ge(s_z, 3 + CREDIT)
                    with dve.Fori(0, REP) as r:
                        link = Link(dve, s_dc, LINKS * r)
                        dve.wait_ge(s_qt, 2 * r + 1 + CREDIT)
                        dve.tensor_copy(qT[0:HD, 0, 0, :], PT[0][0:HD, :])
                        dve.tensor_copy(qT[HD:P, 0, 1, :], PT[0][HD:P, :]).then_inc(s_qd, 1)

                        def maxima(u):
                            bf = u % 4
                            dve.wait_ge(s_s, U * r + u + 1 + CREDIT)
                            link(dve.tensor_reduce(st[:, bf, 0, :], S[u % 2][:, :, 0:(u % NT + 1) * P], AX.X, ALU.max))
                            dve.tensor_scalar(st[:, bf, 1, :], st[:, bf, 0, :], FLOOR, -SCALE, ALU.max, ALU.mult
                                              ).then_inc(s_nm, 1)

                        def copy_pT(u):
                            n = (u % NT + 1) * P
                            dve.wait_ge(s_t, 2 * U * r + 2 * u + 1 + CREDIT)
                            dve.tensor_copy(pT[:, 0, 0:n], PT[0][:, 0:n]).then_inc(s_pd, 1)

                        maxima(0)
                        maxima(1)
                        dve.wait_ge(s_cs, r + 1 + CREDIT)
                        sc = CS.rearrange("p g (t c) -> p g t c", t=NT)[:, :, :, 0:NC]
                        by_tile = [v.rearrange("p (g t) x -> p g t x", g=KVH) for v in
                                   (cx[:, :, 0:NC], bc(cst[:, 0, :], 2, [P, U, NC]))]
                        link(dve.tensor_reduce(cst[:, 0, :].rearrange("p (g t) -> p g t", g=KVH), sc, AX.X, ALU.max))
                        link(dve.tensor_scalar(cst[:, 0, :], cst[:, 0, :], FLOOR, None, ALU.max))
                        dve.tensor_tensor(by_tile[0], sc, by_tile[1], ALU.subtract).then_inc(s_cd, 1)
                        copy_pT(0)
                        dve.wait_ge(s_ce, r + 1 + CREDIT)
                        link(dve.tensor_reduce(cst[:, 0, :], cx[:, :, 0:NC], AX.X, ALU.add))
                        link(dve.tensor_scalar(cst[:, 0, :], cst[:, 0, :], 1e-30, None, ALU.max))
                        link(dve.reciprocal(cst[:, 1, :], cst[:, 0, :]))
                        for g in range(KVH):
                            part = cst[:, 1, g * NT:(g + 1) * NT].unsqueeze(2)
                            ins = dve.tensor_tensor(part, part, rows[:, 0:NT, bass.ds(C_GATE + 3 * REP * g + 3 * r, 1)], ALU.mult)
                        link(ins)
                        dve.tensor_tensor(cx[:, :, 0:NC], cx[:, :, 0:NC], bc(cst[:, 1, :], 2, [P, U, NC]), ALU.mult).then_inc(s_cp, 1)
                        for u in range(U):
                            g, i = divmod(u, NT)
                            bf, sm = u % 2, st[:, u % 4, 2, :]
                            if u + 2 < U:
                                maxima(u + 2)
                            dve.wait_ge(s_ex, U * r + u + 1 + CREDIT)
                            co = st[:, u % 4, 3, :]
                            part = [O[bf][:, j * P + g * HD:j * P + (g + 1) * HD] for j in range(3)]
                            link(dve.reciprocal(co, sm))
                            link(dve.tensor_tensor(co, co, rows[:, i, bass.ds(C_GATE + 3 * REP * g + 3 * r + 1, 2)], ALU.mult))
                            dve.wait_ge(s_pv, U * r + u + 1 + CREDIT)
                            link(dve.tensor_copy(oa[:, bf, :], part[2]))
                            link(dve.scalar_tensor_tensor(oa[:, bf, :], part[0], co[:, 0:1], oa[:, bf, :],
                                                          ALU.mult, ALU.add))
                            dve.scalar_tensor_tensor(o_tok[:, i, bass.ds(g * REP * HD + r * HD, HD)],
                                                     part[1], co[:, 1:2], oa[:, bf, :],
                                                     ALU.mult, ALU.add).then_inc(s_o, 1)
                            if u + 1 < U:
                                copy_pT(u + 1)
                        assert link.n == LINKS, link.n

    def prompt_dilated(self, rows, o_tok):
        nc = self.nc
        U = 2 * NT
        LINKS = 4 * U
        with ExitStack() as s:
            stq = self.sb(s, "pd_staged", [P, 2, 3, NT, P])
            kT = self.sb(s, "pd_kT", [P, 3, TP])
            qT = self.sb(s, "pd_qT", [P, 3, 2, TP])
            ex = self.sb(s, "pd_exp", [P, 2, 3, TP])
            pT = self.sb(s, "pd_pT", [P, 3, TP])
            st = self.sb(s, "pd_stats", [P, 4, 6])
            S12 = [self.ps(s, f"pd_S12_{b}", [P, 2, 512]) for b in range(2)]
            S0 = self.ps(s, "pd_S0", [P, 512])
            PT = self.ps(s, "pd_PT", [P, 2, 512])
            O = self.ps(s, "pd_O", [P, 512])
            OT = O[:, 256:512]
            s_st = self.lsem("pd_staged")
            s_z = self.lsem("pd_qT_zeroed")
            s_qt = self.lsem("pd_qk_transposed")
            s_qc = [self.lsem("pd_qkT_by_dve"), self.lsem("pd_qkT_by_act")]
            s_s = self.lsem("pd_scores_ready")
            s_nm = self.lsem("pd_negmax_ready")
            s_e0 = self.lsem("pd_exp_group0_done")
            s_ex = self.lsem("pd_exp_done")
            s_t = self.lsem("pd_probs_transposed")
            s_pc = [self.lsem("pd_pT_by_dve"), self.lsem("pd_pT_by_act")]
            s_pv = self.lsem("pd_pv_done")
            s_o = self.lsem("pd_o_written")
            s_dc = self.lsem("pd_dve_chain")

            def blocks(i, g):
                return list(range(max(i - 1, 0), i + 1)) if g == 0 else list(range(i + 1))

            self.credit()
            with nc.Block() as block:
                @block.sync
                def _(sp):
                    with sp.Fori(0, 2) as jp:
                        sp.wait_ge(s_qt, 6 * jp + 6 + CREDIT)
                        for j in range(BS // 2):
                            for src, dst in (("cache_dil_w512", "dil512_sample"), ("cache_dil_w128", "dil128_sample"),
                                             ("cache_nsa_win", "nsa_win_sample")):
                                self.move_cache(sp, src, dst, BS // 2 * jp + j)
                    sp.wait_ge(self.s_rows_out, 16 * self.n_rows_out)

                @block.gpsimd
                def _(pool):
                    pool.memset(qT[:, :, :, :], 0.0).then_inc(s_z, 1)
                    with pool.Fori(0, 2) as jp:
                        pool.wait_ge(s_qt, 6 * jp + CREDIT)
                        pool.nop(nofuse=True)
                        for g in range(3):
                            for qk in range(2):
                                c = col_q(g) + qk * DD
                                pool.tensor_copy(stq[:, qk, g], rows[:, 0:NT, bass.ds(c + jp * P, P)]).then_inc(s_st, 1)

                @block.tensor
                def _(pe):
                    pe.wait_ge(s_z, 1 + CREDIT)
                    with pe.Fori(0, 2) as jp:
                        pe.wait_ge(s_pc[0], 2 * U * jp + CREDIT)
                        pe.wait_ge(s_pc[1], U * jp + CREDIT)
                        for m in range(6):
                            g, qk = divmod(m, 2)
                            pe.wait_ge(s_st, 6 * jp + m + 1 + CREDIT)
                            if m >= 2:
                                pe.wait_ge(s_qc[m % 2], 3 * jp + m // 2 + CREDIT)
                            for t in range(NT):
                                ins = pe.transpose(PT[:, m % 2, t * P:(t + 1) * P], stq[:, qk, g, t, :], self.ident[:, :])
                            ins.then_inc(s_qt, 1)

                        def scores(u):
                            hh, i = divmod(u, NT)
                            pe.wait_ge(s_ex, U * jp + max(u - 1, 0) + CREDIT)
                            for g in (1, 2, 0):
                                if g == 0:
                                    pe.wait_ge(s_e0, U * jp + u + CREDIT)
                                kb = blocks(i, g)
                                n = len(kb) * P
                                k0 = kb[0] * P
                                out = S0[:, 0:n] if g == 0 else S12[u % 2][:, g - 1, 0:n]
                                pe.matmul(out, qT[:, g, hh, i * P:(i + 1) * P], kT[:, g, k0:k0 + n], start=True, stop=False)
                                m = self.mask(f"dil{g}")
                                w = m.shape[1]
                                ins = pe.matmul(out, self.ident_b[:, :], m[:, w - n:w], start=False, stop=True)
                            ins.then_inc(s_s, 1)

                        def trans(u):
                            hh, i = divmod(u, NT)
                            pe.wait_ge(s_ex, U * jp + u + 1 + CREDIT)
                            for g in (1, 2, 0):
                                if g == 0:
                                    pe.wait_ge(s_o, U * jp + u + CREDIT)
                                elif g == 1:
                                    pe.wait_ge(s_pc[0], 2 * U * jp + 2 * u + CREDIT)
                                else:
                                    pe.wait_ge(s_pc[1], U * jp + u + CREDIT)
                                out = OT if g == 0 else PT[:, g - 1, :]
                                for a in range(len(blocks(i, g))):
                                    ins = pe.transpose(out[:, a * P:(a + 1) * P], ex[:, u % 2, g, a * P:(a + 1) * P],
                                                       self.ident[:, :])
                                ins.then_inc(s_t, 1)

                        def pv(u):
                            hh, i = divmod(u, NT)
                            first = True
                            pe.wait_ge(s_pc[0], 2 * U * jp + 2 * u + 2 + CREDIT)
                            pe.wait_ge(s_pc[1], U * jp + u + 1 + CREDIT)
                            for g in (1, 2, 0):
                                kb = blocks(i, g)
                                c = col_q(g) + 2 * DD
                                for a, b in enumerate(kb):
                                    ins = pe.matmul(O[:, 0:P], pT[:, g, a * P:(a + 1) * P],
                                                    rows[:, b, bass.ds(c + jp * P, P)], start=first,
                                                    stop=g == 0 and a == len(kb) - 1)
                                    first = False
                            ins.then_inc(s_pv, 1)

                        pe.wait_ge(s_qc[0], 3 * jp + 3 + CREDIT)
                        pe.wait_ge(s_qc[1], 3 * jp + 3 + CREDIT)
                        scores(0)
                        scores(1)
                        trans(0)
                        for u in range(U):
                            if u + 2 < U:
                                scores(u + 2)
                            pv(u)
                            if u + 1 < U:
                                trans(u + 1)

                @block.scalar
                def _(act):
                    with act.Fori(0, 2) as jp:
                        for g in range(3):
                            act.wait_ge(s_qt, 6 * jp + 2 * g + 2 + CREDIT)
                            act.copy(kT[:, g, :], PT[:, 1, :]).then_inc(s_qc[1], 1)

                        def exps(u):
                            hh, i = divmod(u, NT)
                            b = u % 4
                            act.wait_ge(s_nm, U * jp + u + 1 + CREDIT)
                            act.wait_ge(s_t, 3 * U * jp + 3 * max(u - 1, 0) + CREDIT)
                            n0, n = len(blocks(i, 0)) * P, (i + 1) * P
                            act.activation(ex[:, u % 2, 0, 0:n0], S0[:, 0:n0], ACT.Exp, bias=st[:, b, 2:3],
                                           scale=SCALE, accum_out=st[:, b, 3:4]).then_inc(s_e0, 1)
                            act.activation(ex[:, u % 2, 1:3, 0:n], S12[u % 2][:, :, 0:n], ACT.Exp, bias=st[:, b, 2:3],
                                           scale=SCALE, accum_out=st[:, b, 4:5]).then_inc(s_ex, 1)

                        def copy_pT(u):
                            n = (u % NT + 1) * P
                            act.wait_ge(s_t, 3 * U * jp + 3 * u + 2 + CREDIT)
                            act.copy(pT[:, 2, 0:n], PT[:, 1, 0:n]).then_inc(s_pc[1], 1)

                        exps(0)
                        exps(1)
                        copy_pT(0)
                        for u in range(U):
                            if u + 2 < U:
                                exps(u + 2)
                            if u + 1 < U:
                                copy_pT(u + 1)

                @block.vector
                def _(dve):
                    dve.wait_ge(s_z, 1 + CREDIT)
                    with dve.Fori(0, 2) as jp:
                        link = Link(dve, s_dc, LINKS * jp)
                        for g in range(3):
                            dve.wait_ge(s_qt, 6 * jp + 2 * g + 1 + CREDIT)
                            dve.tensor_copy(qT[0:HD, g, 0, :], PT[0:HD, 0, :])
                            dve.tensor_copy(qT[HD:P, g, 1, :], PT[HD:P, 0, :]).then_inc(s_qc[0], 1)

                        def maxima(u):
                            hh, i = divmod(u, NT)
                            b = u % 4
                            n0, n = len(blocks(i, 0)) * P, (i + 1) * P
                            dve.wait_ge(s_s, U * jp + u + 1 + CREDIT)
                            dve.tensor_reduce(st[:, b, 0:1], S0[:, 0:n0], AX.X, ALU.max)
                            link(dve.tensor_reduce(st[:, b, 1:2], S12[u % 2][:, :, 0:n], AX.XY, ALU.max))
                            link(dve.tensor_tensor(st[:, b, 2:3], st[:, b, 0:1], st[:, b, 1:2], ALU.max))
                            dve.tensor_scalar(st[:, b, 2:3], st[:, b, 2:3], -SCALE, None, ALU.mult).then_inc(s_nm, 1)

                        def copy_pT(u):
                            n0, n = len(blocks(u % NT, 0)) * P, (u % NT + 1) * P
                            dve.wait_ge(s_t, 3 * U * jp + 3 * u + 1 + CREDIT)
                            dve.tensor_copy(pT[:, 1, 0:n], PT[:, 0, 0:n]).then_inc(s_pc[0], 1)
                            dve.wait_ge(s_t, 3 * U * jp + 3 * u + 3 + CREDIT)
                            dve.tensor_copy(pT[:, 0, 0:n0], OT[:, 0:n0]).then_inc(s_pc[0], 1)

                        maxima(0)
                        maxima(1)
                        copy_pT(0)
                        for u in range(U):
                            hh, i = divmod(u, NT)
                            b = u % 4
                            if u + 2 < U:
                                maxima(u + 2)
                            dve.wait_ge(s_ex, U * jp + u + 1 + CREDIT)
                            link(dve.tensor_tensor(st[:, b, 5:6], st[:, b, 3:4], st[:, b, 4:5], ALU.add))
                            link(dve.reciprocal(st[:, b, 5:6], st[:, b, 5:6]))
                            dve.wait_ge(s_pv, U * jp + u + 1 + CREDIT)
                            dve.tensor_scalar(o_tok[:, i, bass.ds(QD + hh * HD + jp * P, HD)], O[:, hh * HD:(hh + 1) * HD],
                                              st[:, b, 5:6], None, ALU.mult).then_inc(s_o, 1)
                            if u + 1 < U:
                                copy_pT(u + 1)
                        assert link.n == LINKS, link.n

    def prompt_outputs_transposed(self, o_tok, oT):
        nc = self.nc
        C = (QD + DD) // P
        ix = self.page_rows
        with ExitStack() as s:
            tp = self.ps(s, "ot_tp", [P, 2, 512])
            s_tp, s_ev = self.sem("ot_transposed"), self.sem("ot_copied")
            s_ix = self.sem("page_rows_ready")
            with nc.Block() as block:
                @block.tensor
                def _(pe):
                    for c in range(C):
                        if c >= 2:
                            pe.wait_ge(s_ev, c - 1)
                        for t in range(NT):
                            ins = pe.transpose(tp[:, c % 2, t * P:(t + 1) * P], o_tok[:, t, c * P:(c + 1) * P], self.ident[:, :])
                        ins.then_inc(s_tp, 1)

                @block.vector
                def _(dve):
                    dve.wait_ge(self.s_pages, 8 * 16)
                    dve.tensor_scalar(ix[:, 1, :], ix[:, 0, :], float(PAGE // STRIDE), self.k("chunk_in_page"),
                                      ALU.mult, ALU.add).then_inc(s_ix, 1)
                    for c in range(C):
                        dve.wait_ge(s_tp, c + 1)
                        dve.tensor_copy(oT[:, c, 0:TP], tp[:, c % 2, :]).then_inc(s_ev, 1)

    def sample_queries(self, rows, qrot):
        nc = self.nc
        k = self.k
        t = NT
        with ExitStack() as s:
            row = self.sb(s, "sq_rows", [P, 4, QD])
            red = self.sb(s, "sq_reduced", [P, 4, KVD])
            sel = [self.ps(s, f"sq_selected{j}", [P, 512]) for j in range(4)]
            tr = [self.ps(s, f"sq_turned{j}", [P, 512]) for j in range(2)]
            nk = self.ps(s, "sq_new_k", [P, 8, TS])
            s_nk, s_vn = self.sem("sq_new_k_turned"), self.sem("sq_new_copied")
            s_sel, s_row = self.sem("sq_rows_selected"), self.sem("sq_rows_ready")
            s_tr, s_cp = self.sem("sq_rows_turned"), self.sem("sq_queries_copied")
            s_v = self.sem("sq_dve_chain")
            srcs = [("nsa", rows[:TS, t, 0:QD]), ("nsa", qrot[:TS, t, :])]
            srcs += [("dil", rows[:TS, t, col_q(g):col_q(g) + DD]) for g in range(3)]
            srcs += [("gate", rows[:TS, t, C_GATE:C_DIL])]
            jobs = [(tl, j, kind, src) for tl in range(2) for j, (kind, src) in enumerate(srcs)]
            turned = [n for n, job in enumerate(jobs) if job[2] != "gate"]

            def turns_before(n):
                return sum(m < n for m in turned)

            with nc.Block() as block:
                @block.tensor
                def _(pe):
                    cols = [C_KS, C_KW] + [col_q(g) + DD + ch * P for g in range(3) for ch in range(2)]
                    for j, c in enumerate(cols):
                        ins = pe.transpose(nk[:, j, :], rows[:TS, t, c:c + P], self.ident[:TS, :TS])
                    ins.then_inc(s_nk, 1)
                    for n in range(len(jobs) + 2):
                        if n < len(jobs):
                            tl, j, kind, src = jobs[n]
                            e = k("esel_d" if kind == "dil" else "esel", TS)[:, tl * P:(tl + 1) * P]
                            if n >= 4:
                                pe.wait_ge(s_row, n - 3)
                            pe.matmul(sel[n % 4][:, 0:src.shape[1]], e, src, start=True, stop=True).then_inc(s_sel, 1)
                        if n - 2 in turned:
                            m, kind = n - 2, jobs[n - 2][2]
                            before = turns_before(m)
                            pe.wait_ge(s_row, m + 1)
                            if before >= 2:
                                pe.wait_ge(s_cp, before - 1)
                            for ch in range(1 if kind == "nsa" else 2):
                                ins = pe.transpose(tr[before % 2][:, ch * P:(ch + 1) * P],
                                                   (red[:, m % 4, :] if kind == "nsa" else row[:, m % 4, ch * P:(ch + 1) * P]),
                                                   self.ident[:, :])
                            ins.then_inc(s_tr, 1)

                @block.scalar
                def _(act):
                    for m in turned:
                        tl, j, kind, _ = jobs[m]
                        before = turns_before(m)
                        act.wait_ge(s_tr, before + 1)
                        if kind == "nsa":
                            act.copy(self.qT_nsa[:, tl, j, :], tr[before % 2][:, 0:P]).then_inc(s_cp, 1)
                        else:
                            act.copy(self.qT_dil[:, tl, 2 * (j - 2):2 * (j - 2) + 2, :],
                                     tr[before % 2][:, 0:2 * P].rearrange("p (a r) -> p a r", a=2)).then_inc(s_cp, 1)

                @block.vector
                def _(dve):
                    link = Link(dve, s_v)
                    for n, (tl, j, kind, _) in enumerate(jobs):
                        dve.wait_ge(s_sel, n + 1)
                        if n >= 4 and turns_before(n - 3):
                            dve.wait_ge(s_tr, turns_before(n - 3))
                        r, c, ps = row[:, n % 4], red[:, n % 4, :], sel[n % 4]
                        if kind == "nsa":
                            link(dve.tensor_tensor(r.rearrange("p (h d) -> p h d", h=NH),
                                                   ps[:, :].rearrange("p (h d) -> p h d", h=NH),
                                                   bc(k("hm"), 2, [P, NH, HD]), ALU.mult))
                            dve.tensor_reduce(c.rearrange("p (g d) -> p g d", g=KVH),
                                              r.rearrange("p (g r d) -> p g d r", g=KVH, r=REP),
                                              AX.X, ALU.add).then_inc(s_row, 1)
                        elif kind == "dil":
                            dve.tensor_tensor(r[:, 0:DD].rearrange("p (h d) -> p h d", h=DH),
                                              ps[:, 0:DD].rearrange("p (h d) -> p h d", h=DH),
                                              bc(k("hm_d"), 2, [P, DH, HD]), ALU.mult).then_inc(s_row, 1)
                        else:
                            link(dve.tensor_tensor(r[:, 0:GD].rearrange("p (h x) -> p h x", h=NH),
                                                   ps[:, 0:GD].rearrange("p (h x) -> p h x", h=NH),
                                                   bc(k("hm"), 2, [P, NH, 3]), ALU.mult))
                            dve.tensor_reduce(self.gate_rows[:, tl, :],
                                              r[:, 0:GD].rearrange("p (h x) -> p x h", h=NH), AX.X, ALU.add).then_inc(s_row, 1)
                    dve.wait_ge(s_nk, 1)
                    dve.tensor_copy(self.newkT[:, :, :], nk[:, :, :]).then_inc(s_vn, 1)

                @block.gpsimd
                def _(pool):
                    pool.tensor_copy(self.vnew[:, 0:KVD], rows[:TS, t, C_VS:C_VS + KVD]).then_inc(s_vn, 1)
                    pool.tensor_copy(self.vnew[:, KVD:2 * KVD], rows[:TS, t, C_VW:C_VW + KVD]).then_inc(s_vn, 1)
                    for g in range(3):
                        c = col_q(g) + 2 * DD
                        pool.tensor_copy(self.vnew[:, 2 * KVD + g * DD:2 * KVD + (g + 1) * DD],
                                         rows[:TS, t, c:c + DD]).then_inc(s_vn, 1)

    def sample_dilated(self, oT):
        nc = self.nc
        k = self.k
        win = self.i["cache_nsa_win"][0].rearrange("b t k g d -> b t (k g d)")
        caches = [self.i[f"cache_dil_w{w}"][0].rearrange("b t k h d -> b t (k h d)") for w in WINDOWS]
        with ExitStack() as s:
            kv0 = self.sb(s, "sd_kv0", [P, 4, 2 * DD])
            kv12 = self.sb(s, "sd_kv12", [P, 4, 2, SS, 2 * DD])
            kvw = self.sb(s, "sd_kvw", [P, 4, 4, 2 * KVD])
            kT = self.sb(s, "sd_kT", [P, 6, 512])
            qT = self.sb(s, "sd_qT", [P, 6, P])
            qTw = self.sb(s, "sd_qTw", [P, P])
            qTz = self.sb(s, "sd_qTz", [P, 4, SS, P])
            e = self.sb(s, "sd_scores", [P, 480])
            ew = self.sb(s, "sd_scores_win", [P, 544])
            pT0 = self.sb(s, "sd_pT0", [P, P])
            pTz = self.sb(s, "sd_pTz", [P, 2, SS, P])
            pTn = self.sb(s, "sd_pTn", [TS, 4, P])
            pTw = self.sb(s, "sd_pTw", [P, 512])
            st = self.sb(s, "sd_stats", [P, 8])
            od = self.sb(s, "sd_o", [P, DD])
            Sd = self.ps(s, "sd_Sd", [P, 512])
            Sw = self.ps(s, "sd_Sw", [P, 512])
            Sn = self.ps(s, "sd_Sn", [P, 512])
            tp = [self.ps(s, f"sd_tp{j}", [P, 512]) for j in range(2)]
            tq = self.ps(s, "sd_tq", [P, 512])
            Op = self.ps(s, "sd_O", [P, 512])
            s_l1 = [self.lsem(f"sd_group1_loaded{b}") for b in range(4)]
            s_ld = [self.lsem(f"sd_others_loaded{b}") for b in range(4)]
            s_q = self.lsem("sd_queries_staged")
            s_tp = self.lsem("sd_k_transposed")
            s_ev = [self.lsem("sd_kT_by_dve"), self.lsem("sd_kT_by_act")]
            s_S = [self.lsem(f"sd_scored{m}") for m in range(6)]
            s_new = self.lsem("sd_new_scored")
            s_sm = self.lsem("sd_scores_masked")
            s_nm = self.lsem("sd_negmax_ready")
            s_ex = self.lsem("sd_exp_done")
            s_tp2 = self.lsem("sd_probs_transposed")
            s_pt = self.lsem("sd_pT_copied")
            s_pv = [self.lsem(f"sd_pv_done{b}") for b in range(4)]
            s_om = self.lsem("sd_o_masked")
            s_ot = self.lsem("sd_o_turned")
            s_end = self.lsem("sd_tile_done")
            s_dc = self.lsem("sd_dve_chain")
            GROUPS = [("g1", 0, 4), ("g1", 1, 4), ("g2", 0, 4), ("g2", 1, 4), ("w", 0, 4), ("g0", 0, 2)]

            def k_block(b, m, a):
                kind, ch, _ = GROUPS[m]
                if kind == "w":
                    return kvw[:, b, a, 0:KVD]
                if kind == "g0":
                    return kv0[:, b, a * P:(a + 1) * P]
                return kv12[:, b, int(kind[1]) - 1, a, ch * P:(ch + 1) * P]

            self.credit()
            with nc.Block() as block:
                @block.sync
                def _(sp):
                    with sp.Fori(0, 2) as i:
                        for b in range(4):
                            n = i * 4 + b
                            sp.wait_ge(s_pv[b], i + CREDIT)
                            sp.nop(nofuse=True)
                            sp.dma_start(kv12[:, b, 0], caches[1][bass.ds(n, 1)].rearrange("o (c j) x -> c (o j) x", j=4)).then_inc(s_l1[b], 16)
                            sp.dma_start(kv12[:, b, 1], caches[2][bass.ds(n, 1)].rearrange("o (c j) x -> c (o j) x", j=16)[:, 0:SS, :]).then_inc(s_ld[b], 16)
                            sp.dma_start(kvw[:, b], win[bass.ds(n, 1)].rearrange("o (c j) x -> c (o j) x", j=4)).then_inc(s_ld[b], 16)
                            sp.dma_start(kv0[:, b], caches[0][bass.ds(n, 1)].rearrange("o c x -> c (o x)")).then_inc(s_ld[b], 16)

                @block.tensor
                def _(pe):
                    with pe.Fori(0, 2) as i:
                        def trans(b, m):
                            pe.wait_ge(s_ev[m % 2], 12 * i + 3 * b + m // 2 + CREDIT)
                            for a in range(GROUPS[m][2]):
                                ins = pe.transpose(tp[m % 2][:, a * P:(a + 1) * P], k_block(b, m, a), self.ident[:, :])
                            ins.then_inc(s_tp, 1)

                        def score(b, m):
                            kind, ch, _ = GROUPS[m]
                            pe.wait_ge(s_ev[m % 2], 12 * i + 3 * b + m // 2 + 1 + CREDIT)
                            r0 = slice(32 * b, 32 * b + 32)
                            if kind == "w":
                                ins = pe.matmul(Sw[r0, :], qTw[:, r0], kT[:, m, :], start=True, stop=True)
                            elif kind == "g0":
                                for a in range(2):
                                    ins = pe.matmul(Sd[r0, 0:P], qT[:, a, r0], kT[:, m, a * P:(a + 1) * P],
                                                    start=a == 0, stop=a == 1)
                            else:
                                g = int(kind[1])
                                for j in range(SS):
                                    ins = pe.matmul(Sd[r0, g * P:(g + 1) * P], qTz[:, 2 * (g - 1) + ch, j, r0],
                                                    kT[:, m, j * P:(j + 1) * P], start=ch == 0 and j == 0,
                                                    stop=ch == 1 and j == SS - 1)
                            ins.then_inc(s_S[m], 1)

                        pe.wait_ge(s_q, i + 1 + CREDIT)
                        pe.wait_ge(s_sm, i + CREDIT)
                        for g in range(3):
                            for ch in range(2):
                                pe.matmul(Sd[:, 3 * P + g * TS:3 * P + (g + 1) * TS], qT[:, 2 * g + ch, :],
                                          self.newkT[:, 2 + 2 * g + ch, :], start=ch == 0, stop=ch == 1)
                        pe.matmul(Sn[:, 0:TS], qTw[:, :], self.newkT[:, 1, :], start=True, stop=True).then_inc(s_new, 1)
                        for b in range(4):
                            pe.wait_ge(s_l1[b], 16 * i + 16 + CREDIT)
                            trans(b, 0)
                            for m in range(6):
                                if m == 1:
                                    pe.wait_ge(s_ld[b], 48 * i + 48 + CREDIT)
                                if m < 5:
                                    trans(b, m + 1)
                                score(b, m)
                        pe.wait_ge(s_ex, i + 1 + CREDIT)
                        pe.wait_ge(s_ev[0], 12 * i + 12 + CREDIT)
                        pe.wait_ge(s_ev[1], 12 * i + 12 + CREDIT)
                        for g in range(3):
                            ins = pe.transpose(tp[0][:, g * P:(g + 1) * P], e[:, g * P:(g + 1) * P], self.ident[:, :])
                        ins.then_inc(s_tp2, 1)
                        for a in range(4):
                            ins = pe.transpose(tp[1][:, a * P:(a + 1) * P], ew[:, a * P:(a + 1) * P], self.ident[:, :])
                        ins.then_inc(s_tp2, 1)
                        for g in range(3):
                            pe.transpose(tq[0:TS, g * P:(g + 1) * P], e[:, 3 * P + g * TS:3 * P + (g + 1) * TS], self.ident[:, :])
                        pe.transpose(tq[0:TS, 3 * P:4 * P], ew[:, 512:544], self.ident[:, :]).then_inc(s_tp2, 1)
                        pe.wait_ge(s_pt, 5 * i + 5 + CREDIT)
                        for b in range(4):
                            r0 = slice(32 * b, 32 * b + 32)
                            pe.matmul(Op[r0, 0:DD], pT0[:, r0], kv0[:, b, DD:2 * DD], start=True, stop=False)
                            for g in range(3):
                                pe.matmul(Op[r0, 0:DD], pTn[:, g, r0], self.vnew[:, 2 * KVD + g * DD:2 * KVD + (g + 1) * DD],
                                          start=False, stop=False)
                            for g in range(2):
                                for j in range(SS):
                                    pe.matmul(Op[r0, 0:DD], pTz[:, g, j, r0], kv12[:, b, g, j, DD:2 * DD], start=False,
                                              stop=g == 1 and j == SS - 1)
                            pe.matmul(Op[r0, DD:DD + KVD], pTn[:, 3, r0], self.vnew[:, KVD:2 * KVD], start=True, stop=False)
                            for a in range(4):
                                ins = pe.matmul(Op[r0, DD:DD + KVD], pTw[:, a * P + 32 * b:a * P + 32 * b + 32],
                                                kvw[:, b, a, KVD:2 * KVD], start=False, stop=a == 3)
                            ins.then_inc(s_pv[b], 1)
                        pe.wait_ge(s_om, i + 1 + CREDIT)
                        for ch in range(2):
                            ins = pe.matmul(tq[:, ch * 16:ch * 16 + 16], od[:, ch * P:(ch + 1) * P], k("row_tok_d"),
                                            start=True, stop=True)
                        ins.then_inc(s_ot, 1)

                def copies(eng, copy, which, i):
                    for b in range(4):
                        for m in range(which, 6, 2):
                            w = GROUPS[m][2] * P
                            eng.wait_ge(s_S[m], 4 * i + b + CREDIT)
                            eng.wait_ge(s_tp, 24 * i + 6 * b + m + 1 + CREDIT)
                            copy(kT[:, m, 0:w], tp[m % 2][:, 0:w]).then_inc(s_ev[which], 1)

                @block.scalar
                def _(act):
                    with act.Fori(0, 2) as i:
                        copies(act, act.copy, 1, i)
                        act.wait_ge(s_nm, i + 1 + CREDIT)
                        act.activation(e[:, :], e[:, :], ACT.Exp, bias=st[:, 2:3], scale=SCALE, accum_out=st[:, 4:5])
                        act.activation(ew[:, :], ew[:, :], ACT.Exp, bias=st[:, 3:4], scale=SCALE,
                                       accum_out=st[:, 5:6]).then_inc(s_ex, 1)
                        act.wait_ge(s_tp2, 3 * i + 2 + CREDIT)
                        act.copy(pTw[:, :], tp[1][:, :]).then_inc(s_pt, 1)
                        act.wait_ge(s_tp2, 3 * i + 3 + CREDIT)
                        act.copy(pTn[:, :, :], tq[0:TS, :].rearrange("p (a r) -> p a r", a=4)).then_inc(s_pt, 1)

                @block.vector
                def _(dve):
                    with dve.Fori(0, 2) as i:
                        link = Link(dve, s_dc, 5 * i)
                        dve.wait_ge(s_end, i + CREDIT)
                        dve.tensor_copy(qTw[:, :], self.qT_nsa[:, bass.ds(i, 1), 1, :].rearrange("p o r -> p (o r)"))
                        link(dve.tensor_copy(qT[:, :, :], self.qT_dil[:, bass.ds(i, 1), :, :].rearrange("p o a r -> p (o a) r")))
                        jm = k("jmask").rearrange("p (j r) -> p j r", j=SS)
                        for m in range(4):
                            ins = dve.tensor_tensor(qTz[:, m], bc(qT[:, 2 + m, :], 1, [P, SS, P]), jm, ALU.mult)
                        ins.then_inc(s_q, 1)
                        copies(dve, dve.tensor_copy, 0, i)
                        dve.wait_ge(s_new, i + 1 + CREDIT)
                        for m in range(6):
                            dve.wait_ge(s_S[m], 4 * i + 4 + CREDIT)
                        dve.tensor_tensor(e[:, :], Sd[:, 0:480], k("dil_mask").rearrange("p (t x) -> p t x", t=2)
                                          [:, bass.ds(i, 1), :].rearrange("p o x -> p (o x)"), ALU.add)
                        dve.tensor_copy(ew[:, 0:512], Sw[:, :])
                        link(dve.tensor_tensor(ew[:, 512:544], Sn[:, 0:TS], k("new_mask").rearrange("p (t x) -> p t x", t=2)
                                               [:, bass.ds(i, 1), :].rearrange("p o x -> p (o x)"), ALU.add))
                        first = ew[:, 0:512].rearrange("p (j c) -> p j c", j=4)[:, :, 0]
                        link(dve.tensor_tensor(first, first, k("win_mask"), ALU.add))
                        dve.tensor_reduce(st[:, 0:1], e[:, :], AX.X, ALU.max)
                        dve.tensor_reduce(st[:, 1:2], ew[:, :], AX.X, ALU.max).then_inc(s_sm, 1)
                        dve.wait_ge(s_sm, i + 1 + CREDIT)
                        dve.tensor_scalar(st[:, 2:4], st[:, 0:2], -SCALE, None, ALU.mult).then_inc(s_nm, 1)
                        dve.wait_ge(s_tp2, 3 * i + 1 + CREDIT)
                        dve.tensor_copy(pT0[:, :], tp[0][:, 0:P]).then_inc(s_pt, 1)
                        for g in range(2):
                            dve.tensor_tensor(pTz[:, g], bc(tp[0][:, (g + 1) * P:(g + 2) * P], 1, [P, SS, P]), jm,
                                              ALU.mult).then_inc(s_pt, 1)
                        link(dve.reciprocal(st[:, 6:8], st[:, 4:6]))
                        for b in range(4):
                            dve.wait_ge(s_pv[b], i + 1 + CREDIT)
                        dve.tensor_scalar(self.o_win[:, bass.ds(i, 1), :].rearrange("p o x -> p (o x)"),
                                          Op[:, DD:DD + KVD], st[:, 7:8], None, ALU.mult)
                        link(dve.tensor_scalar(od[:, :], Op[:, 0:DD], st[:, 6:7], None, ALU.mult))
                        dve.tensor_tensor(od[:, :].rearrange("p (h d) -> p h d", h=DH), od[:, :].rearrange("p (h d) -> p h d", h=DH),
                                          bc(k("hm_d"), 2, [P, DH, HD]), ALU.mult).then_inc(s_om, 1)
                        dve.wait_ge(s_ot, i + 1 + CREDIT)
                        dve.tensor_copy(oT[:, QD // P:, bass.ds(TP + 16 * i, 16)],
                                        tq[:, 0:32].rearrange("p (a r) -> p a r", a=2)).then_inc(s_end, 1)
                        assert link.n == 5

    def sample_nsa(self, oT):
        nc = self.nc
        k = self.k
        pages = self.i["cache_nsa_paged"][0].rearrange("n (c p) x g d -> (n c) (p x g d)", p=STRIDE)
        N1 = NCH - 1
        NB = PAST // 64
        KEYS = PAST + TS
        with ExitStack() as s:
            raw = self.sb(s, "sn_raw", [P, 2, STRIDE, 4 * KVD])
            arr = self.sb(s, "sn_arranged", [P, 2, STRIDE, HD])
            kT = self.sb(s, "sn_kT", [P, STRIDE, P])
            vs = self.sb(s, "sn_v", [P, 4, STRIDE, KVD])
            vc = self.sb(s, "sn_vc", [N1, 4, KVD])
            kc = self.sb(s, "sn_kc", [P, N1])
            S = self.sb(s, "sn_scores", [P, KEYS])
            C = self.sb(s, "sn_scores_cmp", [P, N1])
            pT = self.sb(s, "sn_pT", [P, STRIDE + 1, P])
            pTn = self.sb(s, "sn_pTn", [TS, P])
            imp = self.sb(s, "sn_imp", [P, N1])
            rk = self.sb(s, "sn_rank", [P, 4, 32])
            big = self.sb(s, "sn_pairs", [P, 2, 30 * 30])
            qT = self.sb(s, "sn_qT", [P, 2, P])
            st = self.sb(s, "sn_stats", [P, 16])
            orow = self.sb(s, "sn_o_rows", [P, KVD])
            om = self.sb(s, "sn_o_masked", [P, QD])
            ix = self.page_rows
            tp = [self.ps(s, f"sn_tp{j}", [P, 512]) for j in range(2)]
            hp = [self.ps(s, f"sn_hp{j}", [P, 512]) for j in range(2)]
            kp = self.ps(s, "sn_kp", [P, 512])
            ss = [self.ps(s, f"sn_ss{j}", [P, 512]) for j in range(2)]
            mc = self.ps(s, "sn_misc", [P, 512])
            s_z = self.lsem("sn_rank_zeroed")
            s_ic = self.lsem("sn_index_copied")
            s_arr = self.lsem("sn_arranged")
            s_v = self.lsem("sn_v_copied")
            s_raw = [self.sem(f"sn_raw_loaded{j}") for j in range(2)]
            s_tp = self.lsem("sn_transposed")
            s_ev = [self.lsem("sn_copied_by_dve"), self.lsem("sn_copied_by_act")]
            s_S = [self.lsem(f"sn_scored{q}") for q in range(4)]
            s_sev = [self.lsem("sn_scores_by_dve"), self.lsem("sn_scores_by_act")]
            s_cs = self.lsem("sn_cmp_scored")
            s_cse = self.lsem("sn_cmp_scores_copied")
            s_q = self.lsem("sn_queries_staged")
            s_nw = self.lsem("sn_new_scored")
            s_nm = self.lsem("sn_negmax_ready")
            s_ex = self.lsem("sn_exp_done")
            s_pc = self.lsem("sn_p_cmp_ready")
            s_im = self.lsem("sn_importance_summed")
            s_t = self.lsem("sn_probs_transposed")
            s_te = [self.lsem("sn_pT_by_dve"), self.lsem("sn_pT_by_act")]
            s_pv = self.lsem("sn_pv_done")
            s_om = self.lsem("sn_o_masked_ready")
            s_ot = self.lsem("sn_o_turned")
            s_tn = self.lsem("sn_pT_new_copied")
            s_end = self.lsem("sn_tile_done")
            s_dc = self.lsem("sn_dve_chain")
            cb = self.compress_buffers(s, "sn", NCH, tp, hp, kp, s_tp, s_ev, tp_per=12, ev_per=6)
            LINKS = 17

            self.credit()
            with nc.Block() as block:
                @block.gpsimd
                def _(pool):
                    def gather(i, b):
                        if b >= 2:
                            pool.wait_ge(s_tp, 48 * i + 12 * (b - 2) + 4 + CREDIT)
                            pool.nop(nofuse=True)
                            pool.wait_ge(s_arr, 16 * i + 4 * (b - 1) + CREDIT)
                            pool.nop(nofuse=True)
                            pool.wait_ge(s_v, 4 * i + b - 1 + CREDIT)
                            pool.nop(nofuse=True)
                        else:
                            pool.wait_ge(s_tp, 48 * i + CREDIT)
                            pool.nop(nofuse=True)
                            pool.wait_ge(s_arr, 16 * i + CREDIT)
                            pool.nop(nofuse=True)
                            pool.wait_ge(s_v, 4 * i + CREDIT)
                            pool.nop(nofuse=True)
                        pool.tensor_copy(ix[:, 2, b:b + 1], ix[:, 1, bass.ds(4 * i + b, 1)]).then_inc(s_ic, 1)
                        pool.wait_ge(s_ic, 4 * i + b + 1 + CREDIT)
                        pool.nop(nofuse=True)
                        pool.indirect_dma_start(raw[:, b % 2].rearrange("c p x -> c (p x)"), None, pages,
                                                bass.IndirectOffsetOnAxis(ap=ix[:, 2, b:b + 1], axis=0)
                                                ).then_inc(s_raw[b % 2], 16)

                    with pool.Fori(0, 2) as i:
                        gather(i, 0)
                        gather(i, 1)
                        gather(i, 2)
                        gather(i, 3)

                @block.tensor
                def _(pe):
                    with pe.Fori(0, 2) as i:
                        pe.wait_ge(s_q, i + 1 + CREDIT)
                        pe.matmul(mc[:, 0:TS], qT[:, 1, :], self.newkT[:, 0, :], start=True, stop=True).then_inc(s_nw, 1)
                        pe.wait_ge(s_te[0], 3 * i + CREDIT)
                        pe.wait_ge(s_te[1], 2 * i + CREDIT)
                        for b in range(4):
                            r0 = slice(32 * b, 32 * b + 32)

                            def trans(q):
                                pe.wait_ge(s_ev[q % 2], 24 * i + 6 * b + q // 2 + CREDIT)
                                for a in range(4):
                                    ins = pe.transpose(tp[q % 2][:, a * P:(a + 1) * P],
                                                       raw[:, b % 2, 4 * q + a, 2 * KVD:3 * KVD], self.ident[:, :])
                                ins.then_inc(s_tp, 1)

                            def score(q):
                                pe.wait_ge(s_ev[q % 2], 24 * i + 6 * b + q // 2 + 1 + CREDIT)
                                pe.wait_ge(s_sev[q % 2], 8 * i + 2 * b + q // 2 + CREDIT)
                                pe.matmul(ss[q % 2][r0, :], qT[:, 1, r0], kT[:, 4 * q:4 * q + 4, :], start=True,
                                          stop=True).then_inc(s_S[q], 1)

                            pe.wait_ge(s_raw[b % 2], 32 * i + 16 * (b // 2) + 16)
                            trans(0)
                            for q in range(4):
                                if q < 3:
                                    trans(q + 1)
                                score(q)
                            self.compress_pe(pe, cb, lambda kg, j: arr[:, kg % 2, 2 * j:2 * j + 2, :].rearrange("c a d -> c (a d)"),
                                             4 * i + b, lambda kg: pe.wait_ge(s_arr, 16 * i + 4 * b + kg + 1 + CREDIT))
                            pe.wait_ge(cb["s_out"], 8 * i + 2 * b + 2 + CREDIT)
                            pe.wait_ge(s_cse, 5 * i + b + 1 + CREDIT)
                            pe.matmul(mc[r0, 0:N1], qT[:, 0, r0], kc[:, :], start=True, stop=True).then_inc(s_cs, 1)
                        pe.wait_ge(s_pc, i + 1 + CREDIT)
                        pe.matmul(hp[0][:, 0:N1], k("row_group"), C[:, :], start=True, stop=True).then_inc(s_im, 1)
                        for q in (4, 0, 1, 2, 3):
                            n = {4: 0, 0: 1, 1: 0, 2: 2, 3: 1}[q]
                            bank = {4: 0, 0: 0, 1: 1, 2: 0, 3: 1}[q]
                            pe.wait_ge(s_te[bank], (3, 2)[bank] * i + n + CREDIT)
                            pe.wait_ge(s_ev[bank], 24 * i + 24 + CREDIT)
                            if q == 4:
                                pe.transpose(tp[0][0:N1, 0:P], C[:, :], self.ident[:, :]).then_inc(s_t, 1)
                                continue
                            pe.wait_ge(s_ex, 2 * i + 2 + CREDIT)
                            for a in range(4):
                                ins = pe.transpose(tp[bank][:, a * P:(a + 1) * P],
                                                   S[:, (4 * q + a) * P:(4 * q + a + 1) * P], self.ident[:, :])
                            ins.then_inc(s_t, 1)
                        pe.transpose(mc[0:TS, 0:P], S[:, PAST:KEYS], self.ident[:, :]).then_inc(s_t, 1)
                        pe.wait_ge(s_te[0], 3 * i + 3 + CREDIT)
                        pe.wait_ge(s_te[1], 2 * i + 2 + CREDIT)
                        pe.wait_ge(s_tn, i + 1 + CREDIT)
                        pe.wait_ge(s_v, 4 * i + 4 + CREDIT)
                        for b in range(4):
                            r0 = slice(32 * b, 32 * b + 32)
                            for p in range(STRIDE):
                                pe.matmul(kp[r0, 0:KVD], pT[:, p, r0], vs[:, b, p, :], start=p == 0, stop=False)
                            pe.matmul(kp[r0, 0:KVD], pTn[:, r0], self.vnew[:, 0:KVD], start=False, stop=True)
                            ins = pe.matmul(kp[r0, KVD:2 * KVD], pT[0:N1, STRIDE, r0], vc[:, b, :], start=True, stop=True)
                        ins.then_inc(s_pv, 1)
                        pe.wait_ge(s_om, i + 1 + CREDIT)
                        for c in range(4):
                            ins = pe.matmul(hp[1][:, c * 16:c * 16 + 16], om[:, c * P:(c + 1) * P], k("row_tok"), start=True, stop=True)
                        ins.then_inc(s_ot, 1)

                def copies(eng, copy, which, i, b):
                    r0 = slice(32 * b, 32 * b + 32)
                    for q in range(which, 4, 2):
                        eng.wait_ge(s_S[q], 4 * i + b + CREDIT)
                        eng.wait_ge(s_tp, 48 * i + 12 * b + q + 1 + CREDIT)
                        copy(kT[:, 4 * q:4 * q + 4, :], tp[which][:, :].rearrange("p (a c) -> p a c", a=4)).then_inc(s_ev[which], 1)
                        eng.wait_ge(s_S[q], 4 * i + b + 1 + CREDIT)
                        copy(S[r0, q * 512:(q + 1) * 512], ss[which][r0, :]).then_inc(s_sev[which], 1)

                @block.scalar
                def _(act):
                    with act.Fori(0, 2) as i:
                        act.wait_ge(s_t, 6 * i + CREDIT)
                        for b in range(4):
                            copies(act, act.copy, 1, i, b)
                            self.compress_act(act, cb, 4 * i + b)
                            if b == 0:
                                act.wait_ge(s_end, i + CREDIT)
                            act.wait_ge(s_raw[b % 2], 32 * i + 16 * (b // 2) + 16)
                            act.copy(vs[:, b], raw[:, b % 2, :, 3 * KVD:4 * KVD]).then_inc(s_v, 1)
                        act.wait_ge(s_nm, 2 * i + 1 + CREDIT)
                        act.activation(C[:, :], C[:, :], ACT.Exp, bias=st[:, 1:2], scale=SCALE, accum_out=st[:, 2:3]).then_inc(s_ex, 1)
                        act.wait_ge(s_nm, 2 * i + 2 + CREDIT)
                        act.activation(S[:, :], S[:, :], ACT.Exp, bias=st[:, 5:6], scale=SCALE, accum_out=st[:, 6:7]).then_inc(s_ex, 1)
                        for n, q in enumerate((1, 3)):
                            act.wait_ge(s_t, 6 * i + (3, 5)[n] + CREDIT)
                            act.copy(pT[:, 4 * q:4 * q + 4, :], tp[1][:, :].rearrange("p (a c) -> p a c", a=4)).then_inc(s_te[1], 1)

                @block.vector
                def _(dve):
                    dve.memset(rk[:, :, :], 0.0).then_inc(s_z, 1)
                    dve.wait_ge(s_z, 1 + CREDIT)
                    with dve.Fori(0, 2) as i:
                        link = Link(dve, s_dc, LINKS * i)
                        dve.wait_ge(s_end, i + CREDIT)
                        dve.tensor_copy(qT[:, :, :], self.qT_nsa[:, bass.ds(i, 1), :, :].rearrange("p o a r -> p (o a) r")).then_inc(s_q, 1)
                        dve.wait_ge(s_nw, i + 1 + CREDIT)
                        dve.tensor_tensor(S[:, PAST:KEYS], mc[:, 0:TS], k("new_mask").rearrange("p (t x) -> p t x", t=2)
                                          [:, bass.ds(i, 1), :].rearrange("p o x -> p (o x)"), ALU.add).then_inc(s_cse, 1)

                        def arrange(b, kg):
                            dve.wait_ge(s_tp, 48 * i + 12 * b + ((kg - 2) * 2 + 6 if kg > 1 else -2 * (1 - kg) if b > 0 else 0) + CREDIT)
                            dve.wait_ge(s_raw[b % 2], 32 * i + 16 * (b // 2) + 16)
                            dve.tensor_copy(arr[:, kg % 2], raw[:, b % 2, :, kg * HD:(kg + 1) * HD]).then_inc(s_arr, 1)

                        arrange(0, 0)
                        arrange(0, 1)
                        for b in range(4):
                            r0 = slice(32 * b, 32 * b + 32)
                            copies(dve, dve.tensor_copy, 0, i, b)

                            def next_arrangement(kg):
                                if kg < 2:
                                    arrange(b, kg + 2)
                                elif b < 3:
                                    arrange(b + 1, kg - 2)

                            self.compress_dve(dve, cb, 4 * i + b, kc[:, :], vc[:, b, :], next_arrangement)
                            dve.wait_ge(s_cs, 4 * i + b + 1 + CREDIT)
                            dve.tensor_copy(C[r0, :], mc[r0, 0:N1]).then_inc(s_cse, 1)
                        dve.wait_ge(s_cse, 5 * i + 5 + CREDIT)
                        link(dve.tensor_reduce(st[:, 0:1], C[:, :], AX.X, ALU.max))
                        dve.tensor_scalar(st[:, 1:2], st[:, 0:1], -SCALE, None, ALU.mult).then_inc(s_nm, 1)
                        dve.wait_ge(s_ex, 2 * i + 1 + CREDIT)
                        link(dve.reciprocal(st[:, 3:4], st[:, 2:3]))
                        dve.tensor_scalar(C[:, :], C[:, :], st[:, 3:4], None, ALU.mult).then_inc(s_pc, 1)
                        dve.wait_ge(s_im, i + 1 + CREDIT)
                        link(dve.tensor_copy(imp[:, :], hp[0][:, 0:N1]))
                        link(dve.tensor_reduce(rk[:, 0, 0:30], imp[:, 4:124].rearrange("p (n a) -> p n a", a=4), AX.X, ALU.add))
                        link(dve.tensor_tensor(rk[:, 0, 0:30], rk[:, 0, 0:30], imp[:, 3:120:4], ALU.add))
                        v = rk[:, 0, 0:30]
                        mine, other = bc(v, 2, [P, 30, 30]), bc(v, 1, [P, 30, 30])
                        pairs = [big[:, j, :].rearrange("p (n m) -> p n m", n=30) for j in range(2)]
                        dve.tensor_tensor(pairs[0], other, mine, ALU.is_gt)
                        link(dve.tensor_tensor(pairs[1], other, mine, ALU.is_equal))
                        link(dve.tensor_tensor(big[:, 1, :], big[:, 1, :], k("before"), ALU.mult))
                        link(dve.tensor_tensor(big[:, 0, :], big[:, 0, :], big[:, 1, :], ALU.add))
                        link(dve.tensor_reduce(rk[:, 1, 1:31], pairs[0], AX.X, ALU.add))
                        link(dve.tensor_scalar(rk[:, 2, 1:31], rk[:, 1, 1:31], 12.5, NEG, ALU.is_gt, ALU.mult))
                        dve.wait_ge(s_sev[0], 8 * i + 8 + CREDIT)
                        dve.wait_ge(s_sev[1], 8 * i + 8 + CREDIT)
                        sv = S[:, 0:PAST].rearrange("p (a n c) -> p a n c", a=STRIDE, n=NB)
                        bias = bc(bc(rk[:, 2, :], 2, [P, NB, 4]), 1, [P, STRIDE, NB, 4])
                        link(dve.tensor_tensor(sv, sv, bias, ALU.add))
                        link(dve.tensor_reduce(st[:, 4:5], S[:, :], AX.X, ALU.max))
                        dve.tensor_scalar(st[:, 5:6], st[:, 4:5], -SCALE, None, ALU.mult).then_inc(s_nm, 1)
                        dve.wait_ge(s_t, 6 * i + 1 + CREDIT)
                        dve.tensor_copy(pT[0:N1, STRIDE, :], tp[0][0:N1, 0:P]).then_inc(s_te[0], 1)
                        for n, q in enumerate((0, 2)):
                            dve.wait_ge(s_t, 6 * i + (2, 4)[n] + CREDIT)
                            dve.tensor_copy(pT[:, 4 * q:4 * q + 4, :], tp[0][:, :].rearrange("p (a c) -> p a c", a=4)).then_inc(s_te[0], 1)
                        dve.wait_ge(s_t, 6 * i + 6 + CREDIT)
                        dve.tensor_copy(pTn[:, :], mc[0:TS, 0:P]).then_inc(s_tn, 1)
                        dve.tensor_copy(st[:, 8:11], self.gate_rows[:, bass.ds(i, 1), :].rearrange("p o x -> p (o x)"))
                        link(dve.reciprocal(st[:, 7:8], st[:, 6:7]))
                        link(dve.tensor_tensor(st[:, 9:10], st[:, 9:10], st[:, 7:8], ALU.mult))
                        dve.wait_ge(s_pv, i + 1 + CREDIT)
                        link(dve.tensor_scalar(orow[:, :], kp[:, 0:KVD], st[:, 9:10], None, ALU.mult))
                        link(dve.scalar_tensor_tensor(orow[:, :], kp[:, KVD:2 * KVD], st[:, 8:9], orow[:, :], ALU.mult, ALU.add))
                        link(dve.scalar_tensor_tensor(orow[:, :], self.o_win[:, bass.ds(i, 1), :].rearrange("p o x -> p (o x)"),
                                                      st[:, 10:11], orow[:, :], ALU.mult, ALU.add))
                        for g in range(KVH):
                            ins = dve.tensor_tensor(om[:, g * REP * HD:(g + 1) * REP * HD].rearrange("p (r d) -> p r d", r=REP),
                                                    bc(orow[:, g * HD:(g + 1) * HD], 1, [P, REP, HD]),
                                                    bc(k("hm")[:, g * REP:(g + 1) * REP], 2, [P, REP, HD]), ALU.mult)
                        ins.then_inc(s_om, 1)
                        dve.wait_ge(s_ot, i + 1 + CREDIT)
                        dve.tensor_copy(oT[:, 0:4, bass.ds(TP + 16 * i, 16)], hp[1][:, 0:64].rearrange("p (a r) -> p a r", a=4)
                                        ).then_inc(s_end, 1)
                        assert link.n == LINKS, link.n

    def mix(self, oT, x2, gain, h2T):
        nc = self.nc
        w_in = self.i["w_in"][0]
        HT = T // 2
        products = [(2, 4, 16, 0), (3, 2, 20, 4), (0, KD, 0, 0), (1, KD, KD, 0)]
        with ExitStack() as s:
            hT = self.sb(s, "mx_hT", [P, KD, T])
            mixT = self.sb(s, "mx_mixT", [P, KD, T])
            w = self.sb(s, "mx_w", [P, 2, 22, P])
            sg = self.sb(s, "mx_gates", [P, 2, T])
            pr = self.sb(s, "mx_products", [P, 2, T])
            wo = self.sb(s, "mx_w_out", [P, KD, D])
            s_wo = self.sem("mx_w_out_loaded")
            s_x = self.sem("mx_x_loaded")
            s_mt = self.sem("mx_residual_summed")
            s_xr = self.sem("mx_x2_ready")
            s_gain = self.sem("ffn_gain_loaded")
            self.s_router = self.sem("router_inputs_loaded")
            s_z = self.sem("no_token_ready")
            self.s_zs = self.sem("slots_cleared")
            with ExitStack() as q:
                ps = self.ps(q, "mx_ps", [P, 8, 512])
                s_h = self.sem("mx_hT_loaded")
                s_w = [self.lsem(f"mx_w_loaded{u}") for u in range(2)]
                s_wb = [self.lsem(f"mx_branch_w_loaded{u}") for u in range(2)]
                s_p = {p: self.lsem(f"mx_{name}_summed") for p, name in ((0, "gate_nsa"), (2, "branch_nsa"), (3, "branch_dil"))}
                s_used = [self.lsem(f"mx_w_multiplied{u}") for u in range(2)]
                s_f = [self.lsem(f"mx_bank_read{p}") for p in range(4)]
                s_v = self.lsem("mx_dve_chain")
                self.credit()
                with nc.Block() as block:
                    @block.sync
                    def _(sp):
                        def load_branch_w(u, i):
                            m = (2 * i + u) * P
                            sp.wait_ge(s_used[u], i + CREDIT)
                            sp.dma_start(w[:, u, 16:20, :], self.i["w_branch_nsa"][0][:, bass.ds(m, P)]
                                         .rearrange("(k p) c -> p k c", p=P)).then_inc(s_wb[u], 16)
                            sp.dma_start(w[:, u, 20:22, :], self.i["w_branch_dil"][0][:, bass.ds(m, P)]
                                         .rearrange("(k p) c -> p k c", p=P)).then_inc(s_wb[u], 16)

                        def load_gate_w(u, i):
                            m = (2 * i + u) * P
                            for ab in range(2):
                                sp.dma_start(w[:, u, ab * KD:(ab + 1) * KD, :],
                                             w_in[:, bass.ds(C_MRG + ab * D + m, P)].rearrange("(k p) c -> p k c", p=P)
                                             ).then_inc(s_w[u], 16)

                        load_branch_w(0, 0)
                        sp.dma_start(hT[:, :, :], self.hT_d.rearrange("p (k t) -> p k t", k=KD)).then_inc(s_h, 16)
                        load_gate_w(0, 0)
                        load_branch_w(1, 0)
                        load_gate_w(1, 0)
                        with sp.Fori(0, 3) as i:
                            for u in range(2):
                                load_branch_w(u, i + 1)
                                load_gate_w(u, i + 1)
                        sp.dma_start(wo[:, :, :], self.i["w_out"][0].rearrange("(k p) c -> p k c", p=P)).then_inc(s_wo, 16)
                        for t in range(NT + 1):
                            sp.dma_start(x2[:ROWS[t], t, :], self.x_src[t]).then_inc(s_x, 16)
                        sp.dma_start(gain[:, :], self.i["norm_ffn"][0].partition_broadcast(P)).then_inc(s_gain, 16)
                        wr, bias = self.wr, self.router_bias
                        sp.dma_start(wr[:, :, 0:NG], self.i["router_grp_w"][0].rearrange("(k p) g -> p k g", p=P)).then_inc(self.s_router, 16)
                        sp.dma_start(wr[:, :, NG:NG + NE], self.i["router_exp_w"][0].rearrange("(k p) g -> p k g", p=P)).then_inc(self.s_router, 16)
                        sp.dma_start(bias[:, 0:NG], self.i["router_grp_b"][0].partition_broadcast(P)).then_inc(self.s_router, 16)
                        sp.dma_start(bias[:, NG:NG + NE], self.i["router_exp_b"][0].partition_broadcast(P)).then_inc(self.s_router, 16)
                        sp.dma_start(self.rs[:, :], self.c["route"]).then_inc(self.s_router, 16)
                        sp.wait_ge(s_z, 1)
                        sp.dma_start(self.tok_d.rearrange("(p c) o -> p (c o)", p=P), self.no_token[:, :]).then_inc(self.s_zs, 16)

                    @block.tensor
                    def _(pe):
                        with pe.Fori(0, 4) as i:
                            for u in range(2):
                                pe.wait_ge(s_wb[u], 32 * i + 32 + CREDIT)
                                for p, kk, at, c0 in products:
                                    if p == 0:
                                        pe.wait_ge(s_h, 16)
                                        pe.wait_ge(s_w[u], 32 * i + 32 + CREDIT)
                                    pe.wait_ge(s_f[p], 2 * i + u + CREDIT)
                                    src = hT if p < 2 else oT
                                    for half in range(2):
                                        for k in range(kk):
                                            ins = pe.matmul(ps[:, 2 * p + half, 0:HT], w[:, u, at + k, :],
                                                            src[:, c0 + k, half * HT:(half + 1) * HT], start=k == 0, stop=k == kk - 1)
                                    ins.then_inc(s_used[u] if p == 1 else s_p[p], 1)

                    @block.scalar
                    def _(act):
                        with act.Fori(0, 4) as i:
                            for u in range(2):
                                for p in range(2):
                                    if p == 0:
                                        act.wait_ge(s_p[0], 2 * i + u + 1 + CREDIT)
                                    else:
                                        act.wait_ge(s_used[u], i + 1 + CREDIT)
                                    act.wait_ge(s_f[p + 2], 2 * i + u + CREDIT)
                                    act.activation(sg[:, p, :].rearrange("p (a t) -> p a t", a=2),
                                                   ps[:, 2 * p:2 * p + 2, 0:HT], ACT.Sigmoid).then_inc(s_f[p], 1)

                    @block.gpsimd
                    def _(pool):
                        pool.memset(self.no_token[:, :], 0).then_inc(s_z, 1)
                        pool.memset(h2T[:, :, T:(NT + 1) * P], 0.0).then_inc(s_z, 1)

                    @block.vector
                    def _(dve):
                        with dve.Fori(0, 4) as i:
                            for u in range(2):
                                for p in range(2):
                                    dve.wait_ge(s_p[p + 2], 2 * i + u + 1 + CREDIT)
                                    dve.wait_ge(s_f[p], 2 * i + u + 1 + CREDIT)
                                    dve.tensor_tensor(pr[:, p, :].rearrange("p (a t) -> p a t", a=2),
                                                      ps[:, 2 * p + 4:2 * p + 6, 0:HT],
                                                      sg[:, p, :].rearrange("p (a t) -> p a t", a=2), ALU.mult).then_inc(s_f[p + 2], 1)
                                dve.wait_ge(s_f[3], 2 * i + u + 1 + CREDIT)
                                dve.tensor_tensor(mixT[:, bass.ds(2 * i + u, 1), :].rearrange("p o t -> p (o t)"),
                                                  pr[:, 0, :], pr[:, 1, :], ALU.add).then_inc(s_v, 1)
                                dve.wait_ge(s_v, 2 * i + u + 1 + CREDIT)
            with ExitStack() as q:
                ps = self.ps(q, "mo_ps", [P, 8, 512])
                with nc.Block() as block:
                    @block.tensor
                    def _(pe):
                        pe.wait_ge(s_wo, 16)
                        for n in range(2 * (NT + 1)):
                            t, half = divmod(n, 2)
                            if n >= 8:
                                pe.wait_ge(s_xr, n - 7)
                            for k in range(KD):
                                ins = pe.matmul(ps[:ROWS[t], n % 8, :], mixT[:, k, t * P:t * P + ROWS[t]],
                                                wo[:, k, half * 512:(half + 1) * 512], start=k == 0, stop=k == KD - 1)
                            ins.then_inc(s_mt, 1)

                    @block.vector
                    def _(dve):
                        dve.wait_ge(s_x, 16 * (NT + 1))
                        for n in range(2 * (NT + 1)):
                            t, half = divmod(n, 2)
                            dve.wait_ge(s_mt, n + 1)
                            part = x2[:ROWS[t], t, half * 512:(half + 1) * 512]
                            dve.tensor_tensor(part, ps[:ROWS[t], n % 8, :], part, ALU.add).then_inc(s_xr, 1)
            return s_gain

    def route(self, h2T, wt, dest, blk, blk_at, turns):
        nc = self.nc
        r = self.r
        NTT = NT + 1
        L = NG + NE
        with ExitStack() as s:
            def sb(name, shape, dt=F32):
                return self.sb(s, "rt_" + name, shape, dt)

            wr, bias = self.wr, self.router_bias
            lg = sb("logits", [P, NTT, L])
            gx = sb("g_exp", [P, NTT, NG])
            sc = sb("scalars", [P, 8, NTT])
            gc = sb("g_cand", [P, NTT, NG])
            gh = sb("g_onehot", [P, NTT, NG])
            ge = sb("group_logits", [P, NTT, NG, EPG])
            e8 = sb("e_logits", [P, NTT, EPG])
            ec = sb("e_cand", [P, NTT, EPG])
            eh = sb("e_onehot", [P, 2, NTT, EPG])
            oh = sb("onehot", [P, 2, NTT, NE])
            both = sb("both", [P, NTT, NE])
            cnt = sb("count", [P, NE])
            nb = sb("blocks", [P, NE])
            sq = sb("before", [P, NE, NE])
            st = sb("start", [P, NE])
            fs = sb("first_slot", [P, NE])
            at = sb("block_at_f", [1, MAXBLK])
            en = sb("end", [P, NE])
            posn = sb("slot", [P, NTT, NE])
            df = sb("dest_f", [P, 2, NTT])
            be = sb("block_expert_f", [1, MAXBLK, NE])
            bf = sb("block_expert_s", [1, MAXBLK])
            tf = sb("turns_f", [1, MAXBLK // 2])
            tn = sb("turns_n", [1, 1])
            ids = self.token_ids
            ps = self.ps(s, "rt_logits_ps", [P, NTT, L])
            pp = self.ps(s, "rt_pos_ps", [P, NTT + 1, NE])
            s_l = self.sem("rt_logits_summed")
            s_d = self.sem("rt_dve_chain")
            s_sub = self.sem("rt_differences_ready")
            s_e = self.sem("rt_exp_done")
            s_oh = self.sem("rt_onehots_ready")
            s_pp = self.sem("rt_positions_summed")
            s_ds = self.sem("rt_slots_ready")
            self.s_sc = self.sem("tokens_scattered")
            with nc.Block() as block:
                @block.tensor
                def _(pe):
                    pe.wait_ge(self.s_router, 80)
                    for t in range(NTT):
                        for k in range(KD):
                            ins = pe.matmul(ps[:, t, :], h2T[:, k, t * P:(t + 1) * P], wr[:, k, :], start=k == 0, stop=k == KD - 1)
                    ins.then_inc(s_l, 1)
                    pe.wait_ge(s_oh, 1)
                    for t in range(NTT + 1):
                        for u in range(min(t, NTT)):
                            ins = pe.matmul(pp[:, t, :], r("ones"), both[:, u, :], start=u == 0, stop=t == NTT and u == NTT - 1)
                        if t < NTT:
                            ins = pe.matmul(pp[:, t, :], r("earlier"), both[:, t, :], start=t == 0, stop=True)
                    ins.then_inc(s_pp, 1)

                @block.scalar
                def _(act):
                    act.wait_ge(s_sub, 1)
                    act.activation(gx[:, :, :], gx[:, :, :], ACT.Exp).then_inc(s_e, 1)
                    act.wait_ge(s_sub, 2)
                    act.activation(sc[:, 5, :], sc[:, 5, :], ACT.Exp).then_inc(s_e, 1)

                @block.vector
                def _(dve):
                    link = Link(dve, s_d)
                    tt, ts, red = dve.tensor_tensor, dve.tensor_scalar, dve.tensor_reduce

                    def first_of_max(onehot, value, top, cand, order, n):
                        sh = [P, NTT, n]
                        link(red(top, value, AX.X, ALU.max))
                        link(tt(cand, value, bc(top, 2, sh), ALU.is_equal))
                        link(tt(cand, cand, bc(order, 1, sh), ALU.mult))
                        link(red(sc[:, 7, :], cand, AX.X, ALU.max))
                        link(tt(onehot, cand, bc(sc[:, 7, :], 2, sh), ALU.is_equal))

                    dve.tensor_copy(ids[:, :], r("token_id")).then_inc(s_ds, 1)
                    dve.wait_ge(s_l, 1)
                    link(tt(lg[:, :, :], ps[:, :, :], bc(bias[:, :], 1, [P, NTT, L]), ALU.add))
                    g = lg[:, :, 0:NG]
                    first_of_max(gh[:, :, :], g, sc[:, 0, :], gc[:, :, :], r("g_order"), NG)
                    tt(gx[:, :, :], g, bc(sc[:, 0, :], 2, [P, NTT, NG]), ALU.subtract).then_inc(s_sub, 1)
                    link(tt(ge[:, :, :, :], lg[:, :, NG:L].rearrange("p t (g e) -> p t g e", g=NG),
                            bc(gh[:, :, :], 3, [P, NTT, NG, EPG]), ALU.mult))
                    link(red(e8[:, :, :], ge[:, :, :, :].rearrange("p t g e -> p t e g"), AX.X, ALU.add))
                    first_of_max(eh[:, 0], e8[:, :, :], sc[:, 1, :], ec[:, :, :], r("e_order"), EPG)
                    link(dve.scalar_tensor_tensor(e8[:, :, :], eh[:, 0], NEG, e8[:, :, :], ALU.mult, ALU.add))
                    first_of_max(eh[:, 1], e8[:, :, :], sc[:, 2, :], ec[:, :, :], r("e_order"), EPG)
                    tt(sc[:, 5, :], sc[:, 2, :], sc[:, 1, :], ALU.subtract).then_inc(s_sub, 1)
                    for j in range(2):
                        for t in range(NTT):
                            ins = tt(oh[:, j, t, :].rearrange("p (g e) -> p g e", g=NG), bc(gh[:, t, :], 2, [P, NG, EPG]),
                                     bc(eh[:, j, t, :], 1, [P, NG, EPG]), ALU.mult)
                    link(ins)
                    link(tt(both[:, :, :], oh[:, 0], oh[:, 1], ALU.add))
                    tt(both[:, :, :], both[:, :, :], bc(r("is_token"), 2, [P, NTT, NE]), ALU.mult).then_inc(s_oh, 1)
                    dve.wait_ge(s_e, 2)
                    link(red(sc[:, 3, :], gx[:, :, :], AX.X, ALU.add))
                    link(ts(sc[:, 4, :], sc[:, 5, :], 1.0, None, ALU.add))
                    link(tt(sc[:, 4, :], sc[:, 4, :], sc[:, 3, :], ALU.mult))
                    link(dve.reciprocal(wt[:, 0, :], sc[:, 4, :]))
                    link(tt(wt[:, 1, :], wt[:, 0, :], sc[:, 5, :], ALU.mult))
                    dve.wait_ge(s_pp, 1)
                    link(dve.tensor_copy(cnt[:, :], pp[:, NTT, :]))
                    link(ts(nb[:, :], cnt[:, :], 0.5, None, ALU.is_gt))
                    for j in range(1, -(-T // BLK)):
                        link(dve.scalar_tensor_tensor(nb[:, :], cnt[:, :], j * BLK + 0.5, nb[:, :], ALU.is_gt, ALU.add))
                    link(tt(sq[:, :, :], bc(nb[:, :], 1, [P, NE, NE]), r("e_before").rearrange("p (e f) -> p e f", e=NE), ALU.mult))
                    link(red(st[:, :], sq[:, :, :], AX.X, ALU.add))
                    link(tt(en[:, :], st[:, :], nb[:, :], ALU.add))
                    link(tt(sq[:, :, :], bc(cnt[:, :], 1, [P, NE, NE]), r("e_before").rearrange("p (e f) -> p e f", e=NE), ALU.mult))
                    link(red(fs[:, :], sq[:, :, :], AX.X, ALU.add))
                    link(tt(posn[:, :, :], pp[:, 0:NTT, :], bc(fs[:, :], 1, [P, NTT, NE]), ALU.add))
                    for j in range(2):
                        link(tt(oh[:, j], oh[:, j], posn[:, :, :], ALU.mult))
                        link(red(df[:, j, :], oh[:, j], AX.X, ALU.add))
                    dve.tensor_copy(dest[:, :, :], df[:, :, :]).then_inc(s_ds, 1)
                    link(tt(be[:, :, :], bc(en[0:1, :], 1, [1, MAXBLK, NE]), bc(r("block_no")[0:1, :], 2, [1, MAXBLK, NE]), ALU.is_le))
                    link(red(bf[:, :], be[:, :, :], AX.X, ALU.add))
                    link(ts(bf[:, :], bf[:, :], float(NE - 1), None, ALU.min))
                    link(dve.scalar_tensor_tensor(fs[:, :], st[:, :], -float(BLK), fs[:, :], ALU.mult, ALU.add))
                    link(tt(be[:, :, :], bc(bf[:, :], 2, [1, MAXBLK, NE]), bc(r("e_no")[0:1, :], 1, [1, MAXBLK, NE]), ALU.is_equal))
                    link(tt(be[:, :, :], be[:, :, :], bc(fs[0:1, :], 1, [1, MAXBLK, NE]), ALU.mult))
                    link(red(at[:, :], be[:, :, :], AX.X, ALU.add))
                    link(dve.scalar_tensor_tensor(at[:, :], r("block_no")[0:1, :], float(BLK), at[:, :], ALU.mult, ALU.add))
                    dve.tensor_copy(blk_at[:, :], at[:, :])
                    link(tt(tf[:, :], r("block_no")[0:1, 0:MAXBLK:2], en[0:1, NE - 1:NE].to_broadcast([1, MAXBLK // 2]), ALU.is_lt))
                    link(red(tn[:, :], tf[:, :], AX.X, ALU.add))
                    link(ts(tn[:, :], tn[:, :], -1.0, None, ALU.add))
                    dve.tensor_copy(blk[:, :], bf[:, :])
                    dve.tensor_copy(turns[:, :], tn[:, :])

                @block.gpsimd
                def _(pool):
                    pool.wait_ge(s_ds, 2)
                    pool.wait_ge(self.s_zs, 16)
                    for t in range(NT + 1):
                        for j in range(2):
                            pool.indirect_dma_start(self.tok_d, bass.IndirectOffsetOnAxis(ap=dest[:ROWS[t], j, t:t + 1], axis=0),
                                                    self.token_ids[:ROWS[t], t:t + 1], None).then_inc(self.s_sc, 16)

    def experts(self, blk, blk_at, turns):
        nc = self.nc
        up = self.i["expert_w_up"][0]
        down = self.i["expert_w_down"][0]
        B = BLK
        with ExitStack() as s:
            wu = self.sb(s, "ex_w_up", [P, 2, KD, 2 * FF])
            wd = self.sb(s, "ex_w_down", [P, 2, 2, D])
            ix = self.sb(s, "ex_tokens", [B, 2], I32)
            hg = self.sb(s, "ex_h", [B, 2, D])
            hT = self.sb(s, "ex_hT", [P, 2, KD, B])
            sl = self.sb(s, "ex_silu", [B, 2, FF])
            ac = self.sb(s, "ex_act", [B, 2, FF])
            aT = self.sb(s, "ex_actT", [P, 2, 2, B])
            ys = self.sb(s, "ex_y", [B, 2, D])
            tp = self.ps(s, "ex_tp", [P, 2, 512])
            up_ps = self.ps(s, "ex_up_ps", [P, 2, 512])
            tq = self.ps(s, "ex_tq", [P, 512])
            dn_ps = self.ps(s, "ex_down_ps", [P, 2, 512])
            s_wu = [self.lsem(f"ex_w_up_loaded{u}") for u in range(2)]
            s_wd = [self.lsem(f"ex_w_down_loaded{u}") for u in range(2)]
            s_ix = [self.sem(f"ex_tokens_loaded{u}") for u in range(2)]
            s_hg = [self.sem(f"ex_h_gathered{u}") for u in range(2)]
            s_t0 = self.lsem("ex_h_half_transposed")
            s_th = [self.lsem(f"ex_h_transposed{u}") for u in range(2)]
            s_hd, s_ha = self.lsem("ex_hT_by_dve"), self.lsem("ex_hT_by_act")
            s_up = [self.lsem(f"ex_up_done{u}") for u in range(2)]
            s_sl = self.lsem("ex_silu_done")
            s_ac = self.lsem("ex_act_ready")
            s_ta = self.lsem("ex_act_transposed")
            s_at = self.lsem("ex_actT_copied")
            s_dn = [self.lsem(f"ex_down_done{u}") for u in range(2)]
            s_yd, s_ya = self.lsem("ex_y_by_dve"), self.lsem("ex_y_by_act")
            s_y = [self.lsem(f"ex_y_stored{u}") for u in range(2)]
            half_h = [tp[:, h, 0:4 * B].rearrange("p (a r) -> p a r", a=4) for h in range(2)]
            self.credit()
            with nc.Block() as block:
                def last_turn(eng):
                    return eng.value_load(turns[0:1, 0:1], min_val=MINTURNS - 1, max_val=MAXTURNS - 1)

                @block.sync
                def _(sp):
                    def load_weights(u, k):
                        e = sp.value_load(blk[0:1, bass.ds(2 * k + u, 1)], min_val=0, max_val=NE - 1)
                        sp.wait_ge(s_up[u], k + CREDIT)
                        sp.nop(nofuse=True)
                        sp.dma_start(wu[:, u], up[bass.ds(e, 1)].rearrange("o (p k) f -> p (o k) f", p=P)).then_inc(s_wu[u], 16)
                        sp.wait_ge(s_dn[u], k + CREDIT)
                        sp.nop(nofuse=True)
                        sp.dma_start(wd[:, u], down[bass.ds(e, 1)].rearrange("o (p c) f -> p (o c) f", p=P)).then_inc(s_wd[u], 16)

                    m = last_turn(sp)
                    load_weights(0, 0)
                    load_weights(1, 0)
                    with sp.Fori(0, m) as i:
                        load_weights(0, i + 1)
                        load_weights(1, i + 1)

                @block.gpsimd
                def _(pool):
                    def gather(u, k):
                        at = pool.value_load(blk_at[0:1, bass.ds(2 * k + u, 1)], min_val=0, max_val=SLOTS - B)
                        pool.wait_ge(s_th[u], k + CREDIT)
                        pool.nop(nofuse=True)
                        pool.dma_start(ix[:, u:u + 1], self.tok_d[bass.ds(at, B), :]).then_inc(s_ix[u], 16)
                        pool.wait_ge(s_ix[u], 16 * k + 16)
                        pool.nop(nofuse=True)
                        pool.indirect_dma_start(hg[:, u, :], None, self.h2_d,
                                                bass.IndirectOffsetOnAxis(ap=ix[:, u:u + 1], axis=0)).then_inc(s_hg[u], 16)

                    m = last_turn(pool)
                    pool.wait_ge(self.s_sc, 2 * (NT + 1) * 16)
                    gather(0, 0)
                    gather(1, 0)
                    with pool.Fori(0, m) as i:
                        gather(0, i + 1)
                        gather(1, i + 1)

                @block.tensor
                def _(pe):
                    def turn_h(u, k):
                        pe.wait_ge(s_hg[u], 16 * k + 16)
                        for half in range(2):
                            pe.wait_ge((s_hd, s_ha)[half], 2 * k + u + CREDIT)
                            pe.nop(nofuse=True)
                            for c in range(4 * half, 4 * half + 4):
                                ins = pe.transpose(tp[:, half, (c % 4) * B:(c % 4 + 1) * B], hg[:, u, c:D:KD], self.ident[:B, :B])
                            ins.then_inc((s_t0, s_th[u])[half], 1)

                    def up_proj(u, k):
                        pe.wait_ge(s_hd, 2 * k + u + 1 + CREDIT)
                        pe.wait_ge(s_ha, 2 * k + u + 1 + CREDIT)
                        pe.wait_ge(s_wu[u], 16 * k + 16 + CREDIT)
                        for c in range(KD):
                            ins = pe.matmul(up_ps[:B, u, :], hT[:, u, c, :], wu[:, u, c, :], start=c == 0, stop=c == KD - 1)
                        ins.then_inc(s_up[u], 1)

                    def turn_act(u, k):
                        pe.wait_ge(s_ac, 2 * k + u + 1 + CREDIT)
                        pe.wait_ge(s_at, 2 * k + u + CREDIT)
                        pe.nop(nofuse=True)
                        for c in range(2):
                            ins = pe.transpose(tq[:, c * B:(c + 1) * B], ac[:, u, c:FF:2], self.ident[:B, :B])
                        ins.then_inc(s_ta, 1)

                    def down_proj(u, k):
                        pe.wait_ge(s_at, 2 * k + u + 1 + CREDIT)
                        pe.wait_ge(s_wd[u], 16 * k + 16 + CREDIT)
                        pe.wait_ge(s_yd, 2 * k + u + CREDIT)
                        pe.wait_ge(s_ya, 2 * k + u + CREDIT)
                        for half in range(2):
                            for c in range(2):
                                ins = pe.matmul(dn_ps[:B, half, :], aT[:, u, c, :], wd[:, u, c, half * 512:(half + 1) * 512],
                                                start=c == 0, stop=c == 1)
                        ins.then_inc(s_dn[u], 1)

                    m = last_turn(pe)
                    turn_h(0, 0)
                    up_proj(0, 0)
                    turn_h(1, 0)
                    turn_act(0, 0)
                    with pe.Fori(0, m) as i:
                        for u, k in ((1, i), (0, i + 1)):
                            up_proj(u, k)
                            turn_h(1 - u, i + 1)
                            down_proj(1 - u, i)
                            turn_act(u, k)
                    up_proj(1, m)
                    down_proj(0, m)
                    turn_act(1, m)
                    down_proj(1, m)

                @block.scalar
                def _(act):
                    def silu(u, k):
                        act.wait_ge(s_up[u], k + 1 + CREDIT)
                        act.activation(sl[:, u, :], up_ps[:B, u, 0:FF], ACT.Silu).then_inc(s_sl, 1)

                    def copy_h(u, k):
                        act.wait_ge(s_th[u], k + 1 + CREDIT)
                        act.copy(hT[:, u, 4:8, :], half_h[1]).then_inc(s_ha, 1)

                    def copy_act(u, k):
                        act.wait_ge(s_ta, 2 * k + u + 1 + CREDIT)
                        act.copy(aT[:, u, :, :], tq[:, 0:2 * B].rearrange("p (a r) -> p a r", a=2)).then_inc(s_at, 1)

                    def store(u, k):
                        at = act.value_load(blk_at[0:1, bass.ds(2 * k + u, 1)], min_val=0, max_val=SLOTS - B)
                        act.wait_ge(s_dn[u], k + 1 + CREDIT)
                        act.wait_ge(s_y[u], 16 * k + CREDIT)
                        act.copy(ys[:, u, 0:512], dn_ps[:B, 0, :]).then_inc(s_ya, 1)
                        act.wait_ge(s_ya, 2 * k + u + 1 + CREDIT)
                        act.wait_ge(s_yd, 2 * k + u + 1 + CREDIT)
                        act.wait_ge(s_y[1 - u], 16 * (k + u) + CREDIT)
                        act.dma_start(self.y_d[bass.ds(at, B), :], ys[:, u, :]).then_inc(s_y[u], 16)

                    m = last_turn(act)
                    copy_h(0, 0)
                    silu(0, 0)
                    copy_h(1, 0)
                    copy_act(0, 0)
                    with act.Fori(0, m) as i:
                        for u, k in ((1, i), (0, i + 1)):
                            silu(u, k)
                            copy_h(1 - u, i + 1)
                            store(1 - u, i)
                            copy_act(u, k)
                    silu(1, m)
                    store(0, m)
                    copy_act(1, m)
                    store(1, m)
                    for u in range(2):
                        act.wait_ge(s_y[u], 16 * m + 16 + CREDIT)
                        act.nop(nofuse=True)

                @block.vector
                def _(dve):
                    def gate(u, k):
                        dve.wait_ge(s_sl, 2 * k + u + 1 + CREDIT)
                        dve.tensor_tensor(ac[:, u, :], sl[:, u, :], up_ps[:B, u, FF:2 * FF], ALU.mult).then_inc(s_ac, 1)

                    def copy_h(u, k):
                        dve.wait_ge(s_t0, 2 * k + u + 1 + CREDIT)
                        dve.tensor_copy(hT[:, u, 0:4, :], half_h[0]).then_inc(s_hd, 1)

                    def copy_y(u, k):
                        dve.wait_ge(s_dn[u], k + 1 + CREDIT)
                        dve.wait_ge(s_y[u], 16 * k + CREDIT)
                        dve.tensor_copy(ys[:, u, 512:D], dn_ps[:B, 1, :]).then_inc(s_yd, 1)

                    m = last_turn(dve)
                    copy_h(0, 0)
                    gate(0, 0)
                    copy_h(1, 0)
                    with dve.Fori(0, m) as i:
                        for u, k in ((1, i), (0, i + 1)):
                            gate(u, k)
                            copy_h(1 - u, i + 1)
                            copy_y(1 - u, i)
                    gate(1, m)
                    copy_y(0, m)
                    copy_y(1, m)

    def finish(self, x2, wt, dest):
        nc = self.nc
        y_out = [self.o["y_prompt"][0, t * P:(t + 1) * P, :] for t in range(NT)]
        y_out.append(self.o["y_sample"].rearrange("b s d -> (b s) d"))
        with ExitStack() as s:
            yg = self.sb(s, "fi_y", [P, NT + 1, 2, D])
            gain = self.sb(s, "fi_gain", [P, D])
            sq = self.sb(s, "fi_sq", [P, D])
            ms = self.sb(s, "fi_ms", [P, 2, NT + 1])
            s_g = self.sem("fi_gain_loaded")
            s_y = [self.sem(f"fi_y_gathered{t}") for t in range(NT + 1)]
            s_d, s_x, s_r = self.sem("fi_dve_chain"), self.sem("fi_x_ready"), self.sem("fi_rms_ready")
            s_sq, s_o, s_st = self.sem("fi_squared"), self.sem("fi_out_ready"), self.sem("fi_out_stored")
            with nc.Block() as block:
                @block.gpsimd
                def _(pool):
                    for t in range(NT + 1):
                        for j in range(2):
                            pool.indirect_dma_start(yg[:ROWS[t], t, j, :], None, self.y_d[0:2 * T, :],
                                                    bass.IndirectOffsetOnAxis(ap=dest[:ROWS[t], j, t:t + 1], axis=0)).then_inc(s_y[t], 16)

                @block.vector
                def _(dve):
                    link = Link(dve, s_d)

                    def norm(t):
                        n = ROWS[t]
                        dve.wait_ge(s_r, t + 1)
                        link(dve.reciprocal(ms[:n, 1, t:t + 1], ms[:n, 0, t:t + 1]))
                        dve.scalar_tensor_tensor(x2[:n, t, :], x2[:n, t, :], ms[:n, 1, t:t + 1], gain[:n, :],
                                                 ALU.mult, ALU.mult).then_inc(s_o, 1)

                    dve.wait_ge(s_g, 16)
                    for t in range(NT + 1):
                        n = ROWS[t]
                        dve.wait_ge(s_y[t], 32)
                        for j in range(2):
                            ins = dve.scalar_tensor_tensor(x2[:n, t, :], yg[:n, t, j, :], wt[:n, j, t:t + 1], x2[:n, t, :],
                                                           ALU.mult, ALU.add)
                            if j == 0:
                                link(ins)
                            else:
                                ins.then_inc(s_x, 1)
                        if t > 0:
                            norm(t - 1)
                    norm(NT)

                @block.scalar
                def _(act):
                    for t in range(NT + 1):
                        n = ROWS[t]
                        act.wait_ge(s_x, t + 1)
                        act.activation(sq[:n, :], x2[:n, t, :], ACT.Square, accum_out=ms[:n, 0, t:t + 1]).then_inc(s_sq, 1)
                        act.wait_ge(s_sq, t + 1)
                        act.activation(ms[:n, 0, t:t + 1], ms[:n, 0, t:t + 1], ACT.Sqrt, bias=self.eps[:n, :],
                                       scale=1.0 / D).then_inc(s_r, 1)

                @block.sync
                def _(sp):
                    sp.dma_start(gain[:, :], self.i["norm_final"].partition_broadcast(P)).then_inc(s_g, 16)
                    for t in range(NT + 1):
                        sp.wait_ge(s_o, t + 1)
                        sp.dma_start(y_out[t], x2[:ROWS[t], t, :]).then_inc(s_st, 16)
                    sp.wait_ge(s_st, 16 * (NT + 1))
                    sp.wait_ge(self.s_moved, 16 * self.n_moved)


def shape_constants():
    pos = np.concatenate([np.arange(TP), PAST + np.tile(np.arange(SS), BS)]).astype(np.float32)
    inv = (1.0 / (np.float32(500000.0) ** (np.arange(HALF, dtype=np.float32) * np.float32(2.0 / 16)))).astype(np.float32)
    ang = pos[:, None] * inv[None, :]
    cs = np.zeros((P, NT + 1, 2, HALF), np.float32)
    for t in range(NT + 1):
        cs[:ROWS[t], t, 0] = np.cos(ang[t * P:t * P + ROWS[t]])
        cs[:ROWS[t], t, 1] = np.sin(ang[t * P:t * P + ROWS[t]])
    q, k = np.arange(P)[:, None], np.arange(P)[None, :]
    causal = np.where(k <= q, 0, NEG)
    masks = np.zeros((P, MASKS_WIDTH), np.float32)

    def put(name, parts):
        a, n = MASK_AT[name]
        masks[:, a:a + n] = np.concatenate(parts, 1)

    put("causal", [causal])
    put("dil0", [np.where(k >= q, 0, NEG), causal])
    for g, dil in ((1, 4), (2, 16)):
        same = np.where((q - k) % dil == 0, 0, NEG)
        put(f"dil{g}", [same] * (NT - 1) + [np.minimum(same, causal)])
    end = np.arange(32)[None, :] * STRIDE + CBLK - 1
    put("cmp", [np.where(end <= t * P + q, 0, NEG) for t in range(NT)])
    return {"route": route_constants(), "sample": sample_constants(), "cos_sin": cs, "masks": masks, "ident": np.eye(P, dtype=np.float32)}


def sample_constants():
    out = np.zeros((P, K_WIDTH), np.float32)

    def put(name, a):
        c, n = K_AT[name]
        out[:a.shape[0], c:c + n] = a.reshape(a.shape[0], n)

    r = np.arange(P)
    seq, low = r // 32, r % 32
    g, step, rep = low // 16, low // 4 % 4, low % 4
    step_d, head_d, used = low // 4, low % 4, low < 16
    step_d = np.where(used, step_d, 0)
    put("hm", (g * REP + rep)[:, None] == np.arange(NH)[None])
    put("hm_d", (head_d[:, None] == np.arange(DH)[None]) & used[:, None])
    tok = seq * SS + step
    tok_d = seq * SS + step_d
    put("row_tok", tok[:, None] == np.arange(16)[None])
    put("row_tok_d", (tok_d[:, None] == np.arange(16)[None]) & used[:, None])
    tt = np.arange(TS)[:, None, None]
    tl = np.arange(2)[None, :, None]
    put("esel", tt == tl * 16 + tok[None, None, :])
    put("esel_d", (tt == tl * 16 + tok_d[None, None, :]) & used[None, None, :])
    grp = seq * 8 + g * 4 + step
    put("row_group", grp[:, None] == grp[None])
    put("jmask", np.broadcast_to((np.arange(SS)[:, None] == step_d[None]) & used[None], (P, SS, P)))
    new = np.arange(TS)[None, None, :]
    own = new // SS == tl * 4 + seq[:, None, None]
    put("new_mask", np.where(own & (new % SS <= step[:, None, None]), 0, NEG))
    dm = np.zeros((P, 2, 480))
    dm[:, :, 0:P] = np.where(np.arange(P)[None, None] >= step_d[:, None, None], 0, NEG)
    dm[:, :, 3 * P:3 * P + TS] = np.where(own & (new % SS <= step_d[:, None, None]), 0, NEG)
    for j in (1, 2):
        dm[:, :, 3 * P + j * TS:3 * P + (j + 1) * TS] = np.where(own & (new % SS == step_d[:, None, None]), 0, NEG)
    put("dil_mask", dm)
    put("win_mask", np.where(np.arange(4)[None] > step[:, None], 0, NEG))
    n = np.arange(30)
    put("before", np.broadcast_to(n[None, None, :] < n[None, :, None], (P, 30, 30)))
    put("chunk_in_page", (r % 8)[:, None])
    return out


def route_constants():
    out = np.zeros((P, R_WIDTH), np.float32)

    def put(name, a):
        c, n = R_AT[name]
        out[:, c:c + n] = a

    r = np.arange(P)[:, None]
    put("g_order", NG - np.arange(NG)[None])
    put("e_order", EPG - np.arange(EPG)[None])
    put("is_token", r + P * np.arange(NT + 1)[None] < T)
    put("token_id", r + P * np.arange(NT + 1)[None])
    put("ones", 1)
    put("earlier", r < np.arange(P)[None])
    put("e_before", (np.arange(NE)[None, :] < np.arange(NE)[:, None]).reshape(1, -1))
    put("e_no", np.arange(NE)[None])
    put("block_no", np.arange(MAXBLK)[None])
    return out


def decoder_layer(nc, ins, consts, outs):
    with ExitStack() as ctx:
        p = Program(nc, ins, consts, outs, ctx)
        p.hT_d = nc.dram_tensor("hT_scratch", (P, KD * T), F32).ap()
        p.h2_d = nc.dram_tensor("h2_scratch", (T, D), F32).ap()
        p.y_d = nc.dram_tensor("y_scratch", (SLOTS, D), F32).ap()
        p.tok_d = nc.dram_tensor("token_scratch", (SLOTS, 1), I32).ap()
        p.s_moved = nc.alloc_semaphore(name="caches_moved")
        p.n_moved = 4 * BS
        p.s_rows_out = p.sem("rows_stored")
        p.n_rows_out = 0
        p.ident = p.sb(ctx, "ident", [P, P])
        p.eps = p.sb(ctx, "eps", [P, 1])
        oT = p.sb(ctx, "oT", [P, (QD + DD) // P, T])
        sample = ctx.enter_context(ExitStack())
        w_upper = p.parts_place("w_in_upper", [P, 2, KD, WCH])
        sample_place = p.sb(sample, "sample_place", [P, max(2 * KD * WCH, K_WIDTH + 4 * P + 8 * TS + 4 * KVD + 3 * DD)])
        at = 0

        def place_for(width, parts=P):
            nonlocal at
            at += width
            return sample_place[0:parts, at - width:at]

        p.ks = place_for(K_WIDTH)
        p.qT_nsa = place_for(4 * P).rearrange("p (t j r) -> p t j r", t=2, j=2)
        p.newkT = place_for(8 * TS).rearrange("p (c t) -> p c t", c=8)
        p.vnew = place_for(2 * KVD + 3 * DD, TS)
        p.o_win = place_for(2 * KVD).rearrange("p (t c) -> p t c", t=2)
        p.gate_rows = p.sb(sample, "gate_rows", [P, 2, 3])
        p.page_rows = p.sb(sample, "page_rows", [P, 3, BS], I32)
        p.w1 = p.sb(sample, "cmp_w1", [P, 2, 16, P])
        p.w2k = p.sb(sample, "cmp_w2_k", [P, 2, P])
        p.w2v = p.sb(sample, "cmp_w2_v", [P, HD])
        p.peT = p.sb(sample, "cmp_peT", [P, 2, 16])
        p.pe_bias = p.sb(sample, "cmp_pe_bias", [P, 2])
        dilated = sample.enter_context(ExitStack())
        p.qT_dil = p.sb(dilated, "qT_dil", [P, 2, 6, P])
        rows_life = dilated.enter_context(ExitStack())
        p.ident_b = p.sb(rows_life, "ident_bf16", [P, P], BF16)
        p.masks_b = p.sb(rows_life, "masks_bf16", [P, MASKS_WIDTH], BF16)
        p.cs = p.sb(rows_life, "cos_sin", [P, NT + 1, 2, HALF])
        rows = p.sb(rows_life, "rows", [P, NT + 1, C_MRG])
        p.x_src = [ins["x_prompt"][0, t * P:(t + 1) * P, :] for t in range(NT)]
        p.x_src.append(ins["x_sample"].rearrange("b s d -> (b s) d"))
        QR = (NT + 1) * QD
        hT_rest = p.parts_place("hT_rest", [P, KD, T])
        place = p.sb(rows_life, "qrot_and_o_tok", [P, QR + NT * (QD + DD)])
        qrot = place[:, 0:QR].rearrange("p (t c) -> p t c", c=QD)
        o_tok = place[:, QR:QR + NT * (QD + DD)].rearrange("p (t c) -> p t c", c=QD + DD)
        kcT = p.sb(rows_life, "prompt_kcT", [P, NCH_P - 1])
        vc = p.sb(rows_life, "prompt_vc", [NCH_P - 1, KVD])
        with ExitStack() as source:
            pc_src = p.sb(source, "prompt_cmp_source", [NCH_P, 4, STRIDE, HD])
            with ExitStack() as s:
                hT = p.sb(s, "hT_upper", [P, KD, T], F32R)
                p.masks_f, gain = rows[:, 0, 2 * D:2 * D + MASKS_WIDTH], rows[:, 1, 2 * D:3 * D]
                p.pe_rows = rows[0:16, 3, 2 * D:2 * D + 2 * P].rearrange("p (a c) -> p a c", a=2)
                w_rest = p.parts_place("w_in_rest", [P, 2, KD, WCH])
                w = p.sb(s, "w_in_chunk", [P, 2, KD, WCH])
                s_w, s_x, s_gain, beside, tables_loaded = p.first_loads(rows, gain, w)
                s_saved = p.sem("hT_saved")
                split = (hT_rest, lambda t: rows[:, t, 0:KD * ROWS[t]].rearrange("p (k r) -> p k r", k=KD),
                         p.hT_d.rearrange("p (k t) -> p k t", k=KD), s_saved)
                p.norm_transpose("mix", rows[:, :, 0:D], rows[:, :, D:2 * D], rows[:, 2, 2 * D:3 * D], gain,
                                 s_x, s_gain, hT, split=split, **beside)
                p.project(hT, hT_rest, w, w_upper, w_rest, s_w, rows, pc_src, s_saved, tables_loaded)
            p.finish_rows(rows, qrot, pc_src, kcT[:, :], vc[:, :])
        p.prompt_nsa(rows, qrot, kcT, vc, o_tok)
        p.prompt_dilated(rows, o_tok)
        p.prompt_outputs_transposed(o_tok, oT)
        p.clear_semaphores()
        p.sample_queries(rows, qrot)
        rows_life.close()
        p.sample_dilated(oT)
        dilated.close()
        p.sample_nsa(oT)
        sample.close()
        p.clear_semaphores()
        x2 = p.sb(ctx, "x2", [P, NT + 1, D])
        wt = p.sb(ctx, "expert_weight", [P, 2, NT + 1])
        dest = p.sb(ctx, "slot_of_token", [P, 2, NT + 1], I32)
        blk = p.sb(ctx, "block_expert", [1, MAXBLK], I32)
        blk_at = p.sb(ctx, "block_at", [1, MAXBLK], I32)
        turns = p.sb(ctx, "turns_less_one", [1, 1], I32)
        p.token_ids = p.sb(ctx, "token_ids", [P, NT + 1], I32)
        with ExitStack() as s:
            h2T = p.sb(s, "h2T", [P, KD, (NT + 1) * P])
            p.rs = p.sb(s, "route_constants", [P, R_WIDTH])
            p.wr = p.sb(s, "router_w", [P, KD, NG + NE])
            p.router_bias = p.sb(s, "router_bias", [P, NG + NE])
            p.no_token = p.sb(s, "no_token", [P, SLOTS // P], I32)
            gain = p.sb(s, "gain_ffn", [P, D])
            s_gain = p.mix(oT, x2, gain, h2T)
            h2 = p.sb(s, "h2", [P, NT + 1, D])
            squares = p.sb(s, "ffn_squares", [P, D])
            p.norm_transpose("ffn", x2, h2, squares, gain, None, s_gain, h2T, h_store=p.h2_d)
            p.route(h2T, wt, dest, blk, blk_at, turns)
        p.experts(blk, blk_at, turns)
        p.finish(x2, wt, dest)
OUTS = [
    ("y_prompt", (1, TP, D)), ("y_sample", (BS, SS, D)),
    ("nsa_rows_prompt", (1, 1, TP, 4, KVH, HD)), ("nsa_rows_sample", (1, BS, SS, 4, KVH, HD)),
    ("nsa_win_prompt", (1, 1, 512, 2, KVH, HD)), ("nsa_win_sample", (1, BS, 512, 2, KVH, HD)),
    ("dil128_prompt", (1, 1, 128, 2, DH, HD)), ("dil128_sample", (1, BS, 128, 2, DH, HD)),
    ("dil512_prompt", (1, 1, 512, 2, DH, HD)), ("dil512_sample", (1, BS, 512, 2, DH, HD)),
    ("dil2048_prompt", (1, 1, 512, 2, DH, HD)), ("dil2048_sample", (1, BS, 2048, 2, DH, HD)),
]
INS = ["x_prompt", "x_sample", "cache_nsa_paged", "cache_nsa_win", "cache_dil_w128", "cache_dil_w512",
       "cache_dil_w2048", "page_table", "norm_mix", "w_in", "cmp_pe_k", "cmp_w1_k", "cmp_w2_k", "cmp_pe_v",
       "cmp_w1_v", "cmp_w2_v", "w_branch_nsa", "w_branch_dil", "w_out", "norm_ffn", "router_grp_w",
       "router_grp_b", "router_exp_w", "router_exp_b", "expert_w_up", "expert_w_down", "norm_final"]


def kernel(**inputs):
    import concourse.bacc as bacc
    from concourse.bass_utils import run_bass_kernel_spmd
    nc = bacc.Bacc("TRN2", target_bir_lowering=False, num_devices=1)
    arrays, ins, consts, outs = {}, {}, {}, {}
    for name in INS:
        a = np.ascontiguousarray(inputs[name])
        arrays[f"in_{name}"] = a
        ins[name] = nc.dram_tensor(f"in_{name}", a.shape, mybir.dt.from_np(a.dtype), kind="ExternalInput").ap()
    for name, a in shape_constants().items():
        arrays[f"const_{name}"] = a
        consts[name] = nc.dram_tensor(f"const_{name}", a.shape, mybir.dt.from_np(a.dtype),
                                      kind="ExternalInput").ap()
    for name, shape in OUTS:
        outs[name] = nc.dram_tensor(f"out_{name}", shape, F32, kind="ExternalOutput").ap()
    decoder_layer(nc, ins, consts, outs)
    r = run_bass_kernel_spmd(nc, [arrays], core_ids=[0])
    return tuple(r.results[0][f"out_{name}"] for name, _ in OUTS)
```
